# Optimizing a Trainium2 kernel written in Bass

```python
import math
import jax, jax.numpy as jnp
from jax import lax
import numpy as np

D_MODEL = 1024
BATCH = 1
SEQ = 128
DEPTH = 2
DEC_BATCH = 1
DEC_SEQ = 1024
PAST_LEN = 128

GRID_W = 64
N_MIXERS = 2
N_DIFF_LAYERS = (DEPTH + 1) // 2
N_GQA_LAYERS = DEPTH // 2
DIFF_HEADS = 8
DIFF_HEAD_DIM = 64
DIFF_WIDTH = DIFF_HEADS * 2 * DIFF_HEAD_DIM
GQA_HEADS = 16
GQA_KV_HEADS = 4
GQA_GROUP = GQA_HEADS // GQA_KV_HEADS
GQA_HEAD_DIM = 64
GQA_Q_WIDTH = GQA_HEADS * GQA_HEAD_DIM
GQA_KV_WIDTH = GQA_KV_HEADS * GQA_HEAD_DIM
ROPE_DIM = 64
ROPE_THETA = 10000.0
D_FF = 2816
CONV_WIDTH = 3
Q_BLOCK = 128
NORM_EPS = 1e-6
N_MOD = 6

kernel_name = "hybrid_diffattn_gqa_convffn_dit_step"

def rms_norm(x, w):
    xf = x.astype(jnp.float32)
    y = xf * lax.rsqrt(jnp.mean(xf * xf, axis=-1, keepdims=True) + NORM_EPS)
    return (y * w.astype(jnp.float32)).astype(x.dtype)

def axial_rope_tables(n_tokens, dtype):
    n_rows = n_tokens // GRID_W
    row, col = jnp.meshgrid(jnp.arange(n_rows, dtype=jnp.float32),
                            jnp.arange(GRID_W, dtype=jnp.float32), indexing="ij")
    row, col = row.reshape(-1), col.reshape(-1)
    axis_dim = ROPE_DIM // 2
    inv_freq = ROPE_THETA ** (-jnp.arange(0, axis_dim, 2, dtype=jnp.float32) / axis_dim)
    ang_r = row[:, None] * inv_freq
    ang_c = col[:, None] * inv_freq
    ang = jnp.concatenate([ang_r, ang_r, ang_c, ang_c], axis=-1)
    return jnp.cos(ang).astype(dtype), jnp.sin(ang).astype(dtype)

def rotate_half_axial(x):
    a = ROPE_DIM // 2
    h = a // 2
    xr, xc = x[..., :a], x[..., a:]
    rh = lambda u: jnp.concatenate([-u[..., h:], u[..., :h]], axis=-1)
    return jnp.concatenate([rh(xr), rh(xc)], axis=-1)

def apply_rope(x, cos, sin):
    return x * cos + rotate_half_axial(x) * sin

def sweep_query_blocks(block_fn, q):
    *lead, s, d = q.shape
    nb = s // Q_BLOCK
    qb = jnp.moveaxis(q.reshape(*lead, nb, Q_BLOCK, d), -3, 0)
    out = lax.map(block_fn, qb)
    out = jnp.moveaxis(out, 0, -3)
    return out.reshape(*out.shape[:-3], s, out.shape[-1])

def diff_qkv(h, w_qkv, rope):
    b, s, _ = h.shape
    q, k, v = jnp.split(h @ w_qkv, 3, axis=-1)
    heads = lambda t: t.reshape(b, s, DIFF_HEADS, 2 * DIFF_HEAD_DIM).transpose(0, 2, 1, 3)
    q, k, v = heads(q), heads(k), heads(v)
    if rope is not None:
        cos, sin = rope
        def rot(t):
            t5 = t.reshape(b, DIFF_HEADS, s, 2, DIFF_HEAD_DIM)
            return apply_rope(t5, cos[:, None], sin[:, None]).reshape(t.shape)
        q, k = rot(q), rot(k)
    return q, k, v

def diff_attend(q, k, v, lam_params, lam_init, subln_w):
    lp = lam_params.astype(jnp.float32)
    lam = jnp.exp(jnp.sum(lp[0] * lp[1])) - jnp.exp(jnp.sum(lp[2] * lp[3])) + lam_init
    k1, k2 = k[..., :DIFF_HEAD_DIM], k[..., DIFF_HEAD_DIM:]
    scale = DIFF_HEAD_DIM ** -0.5

    def block(qb):
        q1, q2 = qb[..., :DIFF_HEAD_DIM], qb[..., DIFF_HEAD_DIM:]
        p1 = jax.nn.softmax(jnp.einsum("bhqd,bhkd->bhqk", q1, k1).astype(jnp.float32) * scale, axis=-1)
        p2 = jax.nn.softmax(jnp.einsum("bhqd,bhkd->bhqk", q2, k2).astype(jnp.float32) * scale, axis=-1)
        a = (p1 - lam * p2).astype(v.dtype)
        return jnp.einsum("bhqk,bhkd->bhqd", a, v)

    o = sweep_query_blocks(block, q)
    o = rms_norm(o, subln_w) * (1.0 - lam_init)
    b, nh, s, dv = o.shape
    return o.transpose(0, 2, 1, 3).reshape(b, s, nh * dv)

def gqa_qkv(h, w_qkv, q_norm_w, k_norm_w, rope):
    b, s, _ = h.shape
    qkv = h @ w_qkv
    q = qkv[..., :GQA_Q_WIDTH].reshape(b, s, GQA_KV_HEADS, GQA_GROUP, GQA_HEAD_DIM).transpose(0, 2, 3, 1, 4)
    k = qkv[..., GQA_Q_WIDTH:GQA_Q_WIDTH + GQA_KV_WIDTH].reshape(b, s, GQA_KV_HEADS, GQA_HEAD_DIM).transpose(0, 2, 1, 3)
    v = qkv[..., GQA_Q_WIDTH + GQA_KV_WIDTH:].reshape(b, s, GQA_KV_HEADS, GQA_HEAD_DIM).transpose(0, 2, 1, 3)
    q, k = rms_norm(q, q_norm_w), rms_norm(k, k_norm_w)
    if rope is not None:
        cos, sin = rope
        q, k = apply_rope(q, cos, sin), apply_rope(k, cos, sin)
    return q, k, v

def gqa_attend(q, k, v):
    scale = GQA_HEAD_DIM ** -0.5

    def block(qb):
        p = jax.nn.softmax(jnp.einsum("bhgqd,bhkd->bhgqk", qb, k).astype(jnp.float32) * scale, axis=-1)
        return jnp.einsum("bhgqk,bhkd->bhgqd", p.astype(v.dtype), v)

    o = sweep_query_blocks(block, q)
    b, hk, g, s, d = o.shape
    return o.transpose(0, 3, 1, 2, 4).reshape(b, s, hk * g * d)

def conv_ffn(h, w_up, conv_w, conv_b, w_down):
    u = h @ w_up
    s = u.shape[1]
    up = jnp.pad(u, ((0, 0), (1, 1), (0, 0)))
    u = up[:, :s] * conv_w[0] + up[:, 1:s + 1] * conv_w[1] + up[:, 2:s + 2] * conv_w[2] + conv_b
    g, val = jnp.split(u, 2, axis=-1)
    return (jax.nn.silu(g) * val) @ w_down

def adaln_params(cond, mod_w, mod_b):
    m = jax.nn.silu(cond) @ mod_w + mod_b
    return jnp.split(m[:, None, :], N_MOD, axis=-1)

def modulate(x, norm_w, shift, scale):
    return rms_norm(x, norm_w) * (1.0 + scale) + shift

def lambda_init(layer_idx):
    return 0.8 - 0.6 * math.exp(-0.3 * layer_idx)

def setup_inputs(seed: int = 0) -> dict:
    key = jax.random.key(seed)
    ks = jax.random.split(key, 25)
    nrm = lambda k, shape: jax.random.normal(k, shape, jnp.float32)
    dh2 = 2 * DIFF_HEAD_DIM
    return {
        "x_prompt": nrm(ks[0], (BATCH, SEQ, D_MODEL)),
        "x_sample": nrm(ks[1], (DEC_BATCH, DEC_SEQ, D_MODEL)),
        "cache_k_diff": nrm(ks[2], (DEC_BATCH, N_DIFF_LAYERS, DIFF_HEADS, PAST_LEN, dh2)),
        "cache_v_diff": nrm(ks[3], (DEC_BATCH, N_DIFF_LAYERS, DIFF_HEADS, PAST_LEN, dh2)),
        "cache_k_gqa": nrm(ks[4], (DEC_BATCH, N_GQA_LAYERS, GQA_KV_HEADS, PAST_LEN, GQA_HEAD_DIM)),
        "cache_v_gqa": nrm(ks[5], (DEC_BATCH, N_GQA_LAYERS, GQA_KV_HEADS, PAST_LEN, GQA_HEAD_DIM)),
        "c": nrm(ks[6], (DEC_BATCH, D_MODEL)),
        "c_ctx": nrm(ks[7], (D_MODEL,)),
        "mod_w": nrm(ks[8], (DEPTH, D_MODEL, N_MOD * D_MODEL)) * D_MODEL ** -0.5,
        "mod_b": nrm(ks[9], (DEPTH, N_MOD * D_MODEL)) * 0.02,
        "norm_attn": 1.0 + 0.05 * nrm(ks[10], (DEPTH, D_MODEL)),
        "norm_ffn": 1.0 + 0.05 * nrm(ks[11], (DEPTH, D_MODEL)),
        "w_qkv_diff": nrm(ks[12], (N_DIFF_LAYERS, D_MODEL, 3 * DIFF_WIDTH)) * D_MODEL ** -0.5,
        "w_o_diff": nrm(ks[13], (N_DIFF_LAYERS, DIFF_WIDTH, D_MODEL)) * DIFF_WIDTH ** -0.5,
        "lambda_diff": 0.1 * nrm(ks[14], (N_DIFF_LAYERS, 4, DIFF_HEAD_DIM)),
        "subln_diff": 1.0 + 0.05 * nrm(ks[15], (N_DIFF_LAYERS, dh2)),
        "w_qkv_gqa": nrm(ks[16], (N_GQA_LAYERS, D_MODEL, GQA_Q_WIDTH + 2 * GQA_KV_WIDTH)) * D_MODEL ** -0.5,
        "w_o_gqa": nrm(ks[17], (N_GQA_LAYERS, GQA_Q_WIDTH, D_MODEL)) * GQA_Q_WIDTH ** -0.5,
        "q_norm_gqa": 1.0 + 0.05 * nrm(ks[18], (N_GQA_LAYERS, GQA_HEAD_DIM)),
        "k_norm_gqa": 1.0 + 0.05 * nrm(ks[19], (N_GQA_LAYERS, GQA_HEAD_DIM)),
        "w_up": nrm(ks[20], (DEPTH, D_MODEL, 2 * D_FF)) * D_MODEL ** -0.5,
        "conv_w": nrm(ks[21], (DEPTH, CONV_WIDTH, 2 * D_FF)) * CONV_WIDTH ** -0.5,
        "conv_b": nrm(ks[22], (DEPTH, 2 * D_FF)) * 0.02,
        "w_down": nrm(ks[23], (DEPTH, D_FF, D_MODEL)) * D_FF ** -0.5,
        "final_norm": 1.0 + 0.05 * nrm(ks[24], (D_MODEL,)),
    }

def reference(x_prompt, x_sample, cache_k_diff, cache_v_diff, cache_k_gqa, cache_v_gqa, c, c_ctx,
              mod_w, mod_b, norm_attn, norm_ffn, w_qkv_diff, w_o_diff, lambda_diff, subln_diff,
              w_qkv_gqa, w_o_gqa, q_norm_gqa, k_norm_gqa, w_up, conv_w, conv_b, w_down, final_norm):

    def token_mixer(h, l, rope, ctx_kv):
        j = l // N_MIXERS
        if l % N_MIXERS == 0:
            q, k, v = diff_qkv(h, w_qkv_diff[j], rope)
            kk, vv = (k, v) if ctx_kv is None else (jnp.concatenate([ctx_kv[0], k], axis=2),
                                                     jnp.concatenate([ctx_kv[1], v], axis=2))
            o = diff_attend(q, kk, vv, lambda_diff[j], lambda_init(l), subln_diff[j])
            return o @ w_o_diff[j], k, v
        q, k, v = gqa_qkv(h, w_qkv_gqa[j], q_norm_gqa[j], k_norm_gqa[j], rope)
        kk, vv = (k, v) if ctx_kv is None else (jnp.concatenate([ctx_kv[0], k], axis=2),
                                                 jnp.concatenate([ctx_kv[1], v], axis=2))
        o = gqa_attend(q, kk, vv)
        return o @ w_o_gqa[j], k, v

    def layer(x, cond, l, rope, ctx_kv):
        sh_a, sc_a, g_a, sh_f, sc_f, g_f = adaln_params(cond, mod_w[l], mod_b[l])
        o, k, v = token_mixer(modulate(x, norm_attn[l], sh_a, sc_a), l, rope, ctx_kv)
        x = x + g_a * o
        f = conv_ffn(modulate(x, norm_ffn[l], sh_f, sc_f), w_up[l], conv_w[l], conv_b[l], w_down[l])
        return x + g_f * f, k, v

    xp = x_prompt
    kd, vd, kg, vg = [], [], [], []
    for l in range(DEPTH):
        xp, k, v = layer(xp, c_ctx[None, :], l, None, None)
        if l % N_MIXERS == 0:
            kd.append(k); vd.append(v)
        else:
            kg.append(k); vg.append(v)
    y_prompt = rms_norm(xp, final_norm)
    new_k_diff = jnp.stack(kd, axis=1)
    new_v_diff = jnp.stack(vd, axis=1)
    new_k_gqa = jnp.stack(kg, axis=1)
    new_v_gqa = jnp.stack(vg, axis=1)

    xs = x_sample
    rope = axial_rope_tables(xs.shape[1], xs.dtype)
    for l in range(DEPTH):
        j = l // N_MIXERS
        if l % N_MIXERS == 0:
            ctx_kv = (cache_k_diff[:, j], cache_v_diff[:, j])
        else:
            ctx_kv = (cache_k_gqa[:, j], cache_v_gqa[:, j])
        xs, _, _ = layer(xs, c, l, rope, ctx_kv)
    y_sample = rms_norm(xs, final_norm)

    return (y_prompt, y_sample, new_k_diff, new_v_diff, new_k_gqa, new_v_gqa)


_drawn_inputs = setup_inputs


def setup_inputs(seed=0):
    import zlib

    import numpy as np

    out = dict(_drawn_inputs(seed))
    spreads = {}
    factors = {'cache_k_gqa': 5.487, 'cache_v_gqa': 5.064, 'q_norm_gqa': 8.0, 'conv_b': 3.801}
    for name, (base, spread) in spreads.items():
        noise = np.random.default_rng([zlib.crc32(name.encode()), seed]).standard_normal(out[name].shape)
        drawn = base * np.exp(spread * noise) if base else spread * noise
        out[name] = __import__('jax').numpy.asarray(drawn.astype(out[name].dtype))
    for name, factor in factors.items():
        out[name] = (out[name] * factor).astype(out[name].dtype)
    return out
```

```python
from collections import namedtuple
from contextlib import ExitStack

import numpy as np
import concourse.bass as bass
from concourse import mybir

F32 = mybir.dt.float32
F32R = mybir.dt.float32r
ALU = mybir.AluOpType
ACT = mybir.ActivationFunctionType
AX = mybir.AxisListType

P = 128
D = 1024
KC = D // P
NS = 1024
NP = 128
T = NS + NP
TT = T // P
NB = 384
NN = T // NB
PAST = 128
EPS = 1e-6
GRID_W = 64
HEADS = 8
DH = 64
SCALE = DH ** -0.5
KW = PAST + NS + NP
QT = NS // P
NKEY = PAST + NS
D_FF = 2816
FC = D_FF // P
GROUPS = FC // 2
PADT = NS + 1 + NP
WORK = 6
LAMBDA_INIT = 0.2
SH_A, SC_A, G_A, SH_F, SC_F, G_F = (KC * i for i in range(6))
NMOD = 6 * KC


def rope_tables():
    inv = (np.float32(10000.0) ** (-np.arange(0, 32, 2, dtype=np.float32) / np.float32(32))).astype(np.float32)
    t = np.arange(NS)
    row = (t // GRID_W).astype(np.float32)[None, :] * inv[:, None]
    col = (t % GRID_W).astype(np.float32)[None, :] * inv[:, None]
    ang = np.concatenate([row, row, col, col], axis=0).astype(np.float32)
    sign = np.where(np.arange(DH) % 32 < 16, -1.0, 1.0).astype(np.float32)[:, None]
    cos, sin = np.cos(ang).astype(np.float32), (np.sin(ang) * sign).astype(np.float32)
    return np.concatenate([cos, cos], axis=0), np.concatenate([sin, sin], axis=0)


class Ring:

    def __init__(self, before, per_head, names, head):
        self.names = {n: i for i, n in enumerate(names)}
        assert len(self.names) == len(names)
        self.before, self.per_head, self.head = before, per_head, head
        self.index = 0 if head is None else head

    def bank(self, name):
        return WORK + (self.before + self.names[name]) % 2

    def earlier(self, name):
        return self.index * (self.per_head // 2) + (self.before + self.names[name]) // 2

    def done(self, name):
        return self.index * self.per_head + self.before + self.names[name] + 1

    def wait_free(self, eng, free, name):
        n = self.before + self.names[name]
        if self.head is not None or n >= 2:
            eng.wait_ge(free[WORK + n % 2], self.earlier(name))

    def wait_read(self, eng, free, name):
        eng.wait_ge(*self.read(free, name))

    def read(self, free, name):
        return free[self.bank(name)], self.earlier(name) + 1

    def wait_earlier_read(self, eng, free):
        for n in (self.before - 2, self.before - 1):
            eng.wait_ge(free[WORK + n % 2], self.index * (self.per_head // 2) + n // 2 + 1)


def wait_both(eng, first, second):
    values = [w[1] if isinstance(w[1], int) else eng.to_reg(w[1]) for w in (first, second)]
    for (sem, _), value in zip((first, second), values):
        eng.wait_ge(sem, value)


class Chain:

    def __init__(self, eng, sem, value=0):
        self.eng, self.sem, self.value = eng, sem, value

    def __call__(self, ins):
        ins.then_inc(self.sem, 1)
        self.value = self.value + 1
        self.eng.wait_ge(self.sem, self.value)


def chunks(ap):
    return ap.rearrange("(k p) n -> p k n", p=P)


class Shared:
    pass


def build(nc, a):
    ctx = ExitStack()
    g = Shared()
    g.nc, g.a, g.stack, g.norm_sems, g.out_sems, g.ffn_sems = nc, a, ctx, {}, {}, {}
    with ctx:
        sb = lambda n, s, d=F32: ctx.enter_context(nc.sbuf_tensor(n, s, d))
        g.PS = ctx.enter_context(nc.psum_tensor("psum", [P, 8, 512], F32))
        g.ident = sb("ident", [P, P])
        g.ones_d = sb("ones_d", [P, 1])
        g.ones_v = sb("ones_v", [P, 1])
        g.ones_h = sb("ones_h", [P, 2])
        g.half = sb("half", [P, 16])
        g.par = sb("par", [P, 5 * P])
        g.mod = sb("mod", [P, 2 * NMOD, 2])
        g.coef = sb("coef", [P, 4, KC, 2])
        g.lam = sb("lam", [P, 4])
        g.Hh = sb("Hh", [P, KC, T], F32R)
        g.Hl = sb("Hl", [P, KC, T], F32R)
        g.x_save = nc.dram_tensor("x_save", [P, KC, T], F32, kind="Internal").ap()
        g.o_save = nc.dram_tensor("o_save", [HEADS, P, T], F32, kind="Internal").ap()
        g.k_save = nc.dram_tensor("k_save", [2, P, 2, KW], F32, kind="Internal").ap()
        g.v_save = nc.dram_tensor("v_save", [2, P, (KW // P) * P], F32, kind="Internal").ap()
        with ExitStack() as s:
            g.x = s.enter_context(nc.sbuf_tensor("x_a", [P, KC, T], F32))
            phase_input(g)
            phase_norm(g, 0)
        for layer in range(2):
            with ExitStack() as s:
                (phase_diff_attention, phase_gqa_attention)[layer](g)
            with ExitStack() as s:
                g.x = s.enter_context(nc.sbuf_tensor(f"x_{layer}", [P, KC, T], F32))
                phase_out_projection(g, layer)
                phase_norm(g, 2 * layer + 1)
                phase_ffn(g, layer)
                if layer == 0:
                    phase_norm(g, 2)
                else:
                    phase_final(g)


PC_C, PC_CTX, PC_NA, PC_NF, PC_FIN, PC_SUB, PC_QN, PC_KN = 0, 8, 16, 32, 48, 56, 57, 58
PC_MB = P
PC_CW = 2 * P
PC_CB = PC_CW + 2 * 3 * 2 * FC


def scope(g, name, sbufs, sems, shared=None):
    s = ExitStack()
    held = {n: s.enter_context(g.nc.sbuf_tensor(f"{name}_{n}", shape, dt)) for n, (shape, dt) in sbufs.items()}
    for n in sems.split():
        if shared is None:
            held[n] = s.enter_context(g.nc.semaphore(f"{name}_{n}"))
        else:
            if n not in shared:
                shared[n] = g.stack.enter_context(g.nc.semaphore(n))
            held[n] = shared[n]
    return namedtuple("Phase", held)(**held), s


def phase_input(g):
    nc, a, PS = g.nc, g.a, g.PS
    b, stack = scope(g, "in", {
        "rows": ([P, 5, P], F32), "xn": ([P, 3, D], F32), "sc": ([P, KC, 32], F32),
        "mw": ([P, 4, 2048], F32), "mrow": ([P, 2, 512], F32), "lrow": ([P, 4, DH], F32),
        "lprod": ([P, 2, DH], F32), "lsum": ([P, 2], F32), "lexp": ([P, 2], F32)},
        "zeroed rows_in lam_in x_in0 x_in1 x_in2 mw0 mw1 mw2 mw3 const par_t par_e silu x_t x_e mw_used mod_row mod_t mod_e coef"
        " lam_steps lam_exp")
    xin = [b.x_in0, b.x_in1, b.x_in2]
    mw_in = [b.mw0, b.mw1, b.mw2, b.mw3]
    with stack, nc.Block() as block:
        @block.sync
        def _(sp):
            sp.wait_ge(b.zeroed, 1)
            R = b.rows
            loads = [
                (R[PC_C:PC_C + 8, 0, :], a.c.rearrange("b (k p) -> (b k) p", p=P)),
                (R[PC_CTX:PC_CTX + 8, 0, :], a.c_ctx.rearrange("(k p) -> k p", p=P)),
                (R[PC_NA:PC_NA + 16, 0, :], a.norm_attn.rearrange("l (k p) -> (l k) p", p=P)),
                (R[PC_NF:PC_NF + 16, 0, :], a.norm_ffn.rearrange("l (k p) -> (l k) p", p=P)),
                (R[PC_FIN:PC_FIN + 8, 0, :], a.final_norm.rearrange("(k p) -> k p", p=P)),
                (R[PC_SUB:PC_SUB + 1, 0, :], a.subln_diff),
                (R[PC_QN:PC_QN + 1, 0, 0:DH], a.q_norm_gqa), (R[PC_QN:PC_QN + 1, 0, DH:P], a.q_norm_gqa),
                (R[PC_KN:PC_KN + 1, 0, 0:DH], a.k_norm_gqa), (R[PC_KN:PC_KN + 1, 0, DH:P], a.k_norm_gqa),
                (R[0:96, 1, :], a.mod_b.rearrange("l (k p) -> (l k) p", p=P)),
            ]
            cw = a.conv_w.rearrange("l j (m p) -> (l j m) p", p=P)
            cb = a.conv_b.rearrange("l (m p) -> (l m) p", p=P)
            loads += [(R[:, 2, :], cw[0:P, :]), (R[:, 3, :], cw[P:2 * P, :]), (R[0:8, 4, :], cw[2 * P:264, :]),
                      (R[8:96, 4, :], cb)]
            for dst, src in loads:
                sp.dma_start(dst, src).then_inc(b.rows_in, 16)
            sp.dma_start(b.lrow[:, :, :].rearrange("p a d -> p (a d)"),
                         a.lambda_diff.rearrange("l a d -> (l a d)").partition_broadcast(P)).then_inc(b.lam_in, 16)
            for s in range(6):
                for k in range(KC):
                    i = s * KC + k
                    if i >= 4:
                        sp.wait_ge(b.mw_used, i - 3)
                    sp.dma_start(b.mw[:, i % 4, :], a.mod_w[s // 3, k * P:(k + 1) * P, (s % 3) * 2048:(s % 3 + 1) * 2048])\
                        .then_inc(mw_in[i % 4], 16)

        @block.scalar
        def _(act):
            act.wait_ge(b.par_e, 1)
            for cond, col in ((0, PC_C), (1, PC_CTX)):
                last = act.activation(b.sc[:, :, cond], g.par[:, col:col + KC], ACT.Silu)
            last.then_inc(b.silu, 1)
            for s in range(6):
                act.wait_ge(b.mw_used, KC * (s + 1))
                if s >= 2:
                    act.wait_ge(b.mod_t, s - 1)
                act.activation(b.mrow[:, s % 2, :], PS[:, 2 + s % 2, :], ACT.Copy).then_inc(b.mod_row, 1)
            act.wait_ge(b.lam_steps, 3)
            act.activation(b.lexp[:, :], b.lsum[:, :], ACT.Exp).then_inc(b.lam_exp, 1)

        @block.gpsimd
        def _(pool):
            pool.memset(b.rows[:, :, :], 0.0).then_inc(b.zeroed, 1)
            pool.memset(g.ident[:, :], 0.0).then_inc(b.const, 1)
            pool.memset(b.sc[:, :, :], 0.0).then_inc(b.const, 1)
            pool.memset(g.ones_d[:, :], 1.0 / D).then_inc(b.const, 1)
            pool.memset(g.ones_v[:, :], 1.0 / P).then_inc(b.const, 1)
            pool.memset(g.half[:, :], -0.5).then_inc(b.const, 1)
            pool.memset(g.ones_h[:, :], 0.0).then_inc(b.const, 1)
            pool.wait_ge(b.const, 6)
            pool.affine_select(out=g.ident[:, :], in_=g.ident[:, :], compare_op=ALU.not_equal, fill=1.0,
                               base=0, pattern=[[-1, P]], channel_multiplier=1).then_inc(b.const, 1)
            pool.wait_ge(b.const, 7)
            pool.memset(g.ones_h[0:DH, 0:1], 1.0 / DH).then_inc(b.const, 1)
            pool.wait_ge(b.const, 8)
            pool.memset(g.ones_h[DH:P, 1:2], 1.0 / DH).then_inc(b.const, 1)
            for t in range(TT):
                if t >= 3:
                    pool.wait_ge(b.x_t, 2 * (t - 2))
                src = a.x_sample[0, t * P:(t + 1) * P, :] if t < QT else a.x_prompt[0, :, :]
                pool.dma_start(b.xn[:, t % 3, :], src).then_inc(xin[t % 3], 16)

        @block.tensor
        def _(pe):
            pe.wait_ge(b.const, 9)
            pe.wait_ge(b.rows_in, 16 * 15)
            for i in range(5):
                last = pe.transpose(PS[:, i // 4, (i % 4) * P:(i % 4 + 1) * P], b.rows[:, i, :], g.ident[:, :])
            last.then_inc(b.par_t, 1)

            def x_tile(t):
                pe.wait_ge(xin[t % 3], 16 * (t // 3 + 1))
                for hf in range(2):
                    if t:
                        pe.wait_ge(b.x_e, 2 * (t - 1) + hf + 1)
                    for k in range(4):
                        last = pe.transpose(PS[:, 4 + hf, k * P:(k + 1) * P],
                                            b.xn[:, t % 3, (4 * hf + k) * P:(4 * hf + k + 1) * P], g.ident[:, :])
                    last.then_inc(b.x_t, 1)

            for t in range(3):
                x_tile(t)
            pe.wait_ge(b.silu, 1)
            for s in range(6):
                if s >= 2:
                    pe.wait_ge(b.mod_row, s - 1)
                for k in range(KC):
                    i = s * KC + k
                    pe.wait_ge(mw_in[i % 4], 16 * (i // 4 + 1))
                    for j in range(4):
                        last = pe.matmul(PS[32 * j:32 * j + 32, 2 + s % 2, :], b.sc[:, k, :],
                                         b.mw[:, i % 4, j * 512:(j + 1) * 512], start=k == 0, stop=k == KC - 1)
                    last.then_inc(b.mw_used, 1)
                if s < 6 and 3 + s < TT:
                    x_tile(3 + s)
                pe.wait_ge(b.mod_row, s + 1)
                if s >= 1:
                    pe.wait_ge(b.mod_e, 2 * s)
                for k in range(4):
                    last = pe.transpose(PS[:, 6, k * P:(k + 1) * P], b.mrow[:, s % 2, k * P:(k + 1) * P], g.ident[:, :])
                last.then_inc(b.mod_t, 1)

        @block.vector
        def _(dve):
            dve.wait_ge(b.par_t, 1)
            dve.tensor_copy(g.par[:, 0:4 * P], PS[:, 0, :])
            dve.tensor_copy(g.par[:, 4 * P:5 * P], PS[:, 1, 0:P]).then_inc(b.par_e, 1)

            def x_tile(t):
                for hf in range(2):
                    dve.wait_ge(b.x_t, 2 * t + hf + 1)
                    dve.tensor_copy(g.x[:, 4 * hf:4 * hf + 4, t * P:(t + 1) * P],
                                    PS[:, 4 + hf, :].rearrange("p (k q) -> p k q", k=4)).then_inc(b.x_e, 1)

            for t in range(3):
                x_tile(t)
            dve.wait_ge(b.par_e, 1)
            for s in range(6):
                if 3 + s < TT:
                    x_tile(3 + s)
                dve.wait_ge(b.mod_t, s + 1)
                for cond in range(2):
                    dve.tensor_tensor(
                        g.mod[:, 16 * s:16 * s + 16, cond].rearrange("p (j k) -> p j k", j=4),
                        PS[:, 6, :].rearrange("p (k j c) -> p c j k", k=4, j=4)[:, cond],
                        g.par[:, PC_MB + 16 * s:PC_MB + 16 * s + 16].rearrange("p (j k) -> p j k", j=4),
                        ALU.add).then_inc(b.mod_e, 1)
            dve.wait_ge(b.mod_e, 12)
            for i in range(4):
                layer, ffn = i // 2, i % 2
                sc = NMOD * layer + (SC_F if ffn else SC_A)
                w = (PC_NF if ffn else PC_NA) + KC * layer
                for cond in range(2):
                    dve.scalar_tensor_tensor(g.coef[:, i, :, cond], g.mod[:, sc:sc + KC, cond], 1.0,
                                             g.par[:, w:w + KC], ALU.add, ALU.mult)
            dve.wait_ge(b.lam_in, 16)
            lam = Chain(dve, b.lam_steps)
            lr = b.lrow[:, :, :].rearrange("p (a c) d -> p a c d", c=2)
            lam(dve.tensor_tensor(b.lprod[:, :, :], lr[:, :, 0, :], lr[:, :, 1, :], ALU.mult))
            lam(dve.reduce_sum(b.lsum[:, 0:1], b.lprod[:, 0, :], AX.X))
            lam(dve.reduce_sum(b.lsum[:, 1:2], b.lprod[:, 1, :], AX.X))
            dve.wait_ge(b.lam_exp, 1)
            dve.scalar_tensor_tensor(g.lam[:, 0:1], b.lexp[:, 1:2], -LAMBDA_INIT, b.lexp[:, 0:1],
                                     ALU.add, ALU.subtract)


def phase_norm(g, which):
    nc, PS = g.nc, g.PS
    layer, ffn = which // 2, which % 2
    shift = NMOD * layer + (SH_F if ffn else SH_A)
    b, stack = scope(g, f"nm{which}", {
        "sq": ([P, 2, T], F32), "acc": ([P, T], F32), "ms": ([P, TT], F32), "r": ([P, TT], F32),
        "xr": ([P, 2, T], F32), "full": ([P, 2, T], F32)},
        "sq_d acc_d stat ms_d r_d bc xr_d full_d hi_d lo_d saved", g.norm_sems)
    k0, a0 = KC * which, (KC - 1) * which
    segments = ((0, NS, 0), (NS, T, 1))
    with stack, nc.Block() as block:
        @block.scalar
        def _(act):
            for k in range(KC):
                if k >= 2:
                    act.wait_ge(b.acc_d, a0 + max(1, k - 2))
                act.activation(b.sq[:, k % 2, :], g.x[:, k, :], ACT.Square).then_inc(b.sq_d, 1)
            for k in range(KC):
                act.wait_ge(b.xr_d, k0 + k + 1)
                for lo, hi, cond in segments:
                    last = act.activation(g.Hh[:, k, lo:hi], b.xr[:, k % 2, lo:hi], ACT.Identity,
                                          bias=g.mod[:, shift + k, cond:cond + 1], scale=g.coef[:, which, k, cond:cond + 1])
                last.then_inc(b.hi_d, 1)

        @block.vector
        def _(dve):
            for k in range(1, KC):
                dve.wait_ge(b.sq_d, k0 + k + 1)
                if k >= 2:
                    dve.wait_ge(b.acc_d, a0 + k - 1)
                dve.tensor_tensor(b.acc[:, :], b.sq[:, 0, :] if k == 1 else b.acc[:, :], b.sq[:, k % 2, :],
                                  ALU.add).then_inc(b.acc_d, 1)
            dve.wait_ge(b.stat, which + 1)
            dve.tensor_scalar(b.ms[:, :], PS[:, 0, 0:TT], EPS, None, ALU.add).then_inc(b.ms_d, 1)
            dve.wait_ge(b.bc, which + 1)
            for k in range(KC):
                if k >= 2:
                    dve.wait_ge(b.hi_d, k0 + k - 1)
                    dve.wait_ge(b.lo_d, k0 + k - 1)
                dve.tensor_tensor(b.xr[:, k % 2, :].rearrange("p (n t) -> p n t", n=NN),
                                  g.x[:, k, :].rearrange("p (n t) -> p n t", n=NN), PS[:, 1:1 + NN, 0:NB],
                                  ALU.mult).then_inc(b.xr_d, 1)
                dve.wait_ge(b.xr_d, k0 + k + 1)
                for lo, hi, cond in segments:
                    last = dve.tensor_scalar(b.full[:, k % 2, lo:hi], b.xr[:, k % 2, lo:hi],
                                             g.coef[:, which, k, cond:cond + 1], g.mod[:, shift + k, cond:cond + 1],
                                             ALU.mult, ALU.add)
                last.then_inc(b.full_d, 1)

        @block.gpsimd
        def _(pool):
            pool.wait_ge(b.ms_d, which + 1)
            pool.tensor_tensor(b.r[:, :], b.ms[:, :], g.half[:, 0:TT], ALU.pow).then_inc(b.r_d, 1)
            for k in range(KC):
                pool.wait_ge(b.full_d, k0 + k + 1)
                pool.wait_ge(b.hi_d, k0 + k + 1)
                pool.tensor_tensor(g.Hl[:, k, :], b.full[:, k % 2, :], g.Hh[:, k, :].bitcast(F32), ALU.subtract)\
                    .then_inc(b.lo_d, 1)

        @block.tensor
        def _(pe):
            pe.wait_ge(b.acc_d, a0 + KC - 1)
            for t in range(TT):
                last = pe.matmul(PS[:, 0, t:t + 1], b.acc[:, t * P:(t + 1) * P], g.ones_d[:, :], start=True, stop=True)
            last.then_inc(b.stat, 1)
            pe.wait_ge(b.r_d, which + 1)
            for t in range(TT):
                last = pe.matmul(PS[:, 1 + t // 3, (t % 3) * P:(t % 3 + 1) * P], b.r[:, t:t + 1].to_broadcast([P, P]),
                                 g.ident[:, :], start=True, stop=True)
            last.then_inc(b.bc, 1)

        @block.sync
        def _(sp):
            if not ffn:
                sp.dma_start(g.x_save, g.x[:, :, :]).then_inc(b.saved, 16)
                sp.wait_ge(b.saved, 16 * (layer + 1))


def product(pe, out, w_hi, w_lo, m_hi, m_lo, start, stop):
    pe.matmul(out, w_hi, m_hi, start=start, stop=False)
    pe.matmul(out, w_lo, m_hi, start=False, stop=False)
    return pe.matmul(out, w_hi, m_lo, start=False, stop=stop)


def linear_bank(g, pe, bank, wh, wl, n):
    for k in range(KC):
        last = product(pe, g.PS[:, bank, 0:NB], wh[:, k, :], wl[:, k, :], g.Hh[:, k, n * NB:(n + 1) * NB],
                       g.Hl[:, k, n * NB:(n + 1) * NB], k == 0, k == KC - 1)
    return last


def phase_out_projection(g, layer):
    nc, PS = g.nc, g.PS
    w_o = (g.a.w_o_diff, g.a.w_o_gqa)[layer][0]
    gate = NMOD * layer + G_A
    b, stack = scope(g, f"wo{layer}", {
        "o": ([P, 2, T], F32), "wr": ([P, 2, KC, P], F32), "wh": ([P, 2, KC, P], F32R), "wl": ([P, 2, KC, P], F32R)},
        "x_in o_in0 o_in1 w_in0 w_in1 o_hi o_lo w_hi w_lo mm added", g.out_sems)
    k0, b0, i0 = KC * layer, NN * KC * layer, 16 * 4 * layer
    o_in, w_in = [b.o_in0, b.o_in1], [b.w_in0, b.w_in1]
    with stack, nc.Block() as block:
        @block.sync
        def _(sp):
            for k in range(HEADS):
                if k >= 2:
                    sp.wait_ge(b.o_lo, k0 + k - 1)
                sp.dma_start(b.o[:, k % 2, :], g.o_save[k]).then_inc(o_in[k % 2], 16)
            sp.dma_start(g.x[:, :, :], g.x_save).then_inc(b.x_in, 16)

        @block.scalar
        def _(act):
            def w_load(m):
                if layer == 0:
                    act.dma_start(b.wr[:, m % 2, :, :], chunks(w_o)[:, :, m * P:(m + 1) * P]).then_inc(w_in[m % 2], 16)
                    return
                rows = w_o.rearrange("(p u i d) n -> u d p i n", p=2, u=2, i=4)
                for u in range(2):
                    for p in range(2):
                        act.dma_start(b.wr[u * DH:(u + 1) * DH, m % 2, 4 * p:4 * p + 4, :],
                                      rows[u, :, p, :, m * P:(m + 1) * P]).then_inc(w_in[m % 2], 16)

            def w_hi(m):
                act.wait_ge(w_in[m % 2], i0 + (16 if layer == 0 else 64) * (m // 2 + 1))
                if m >= 2:
                    act.wait_ge(b.mm, b0 + 3 * (m - 1))
                act.activation(b.wh[:, m % 2, :, :], b.wr[:, m % 2, :, :], ACT.Copy).then_inc(b.w_hi, 1)

            w_load(0)
            w_load(1)
            w_hi(0)
            w_hi(1)
            for k in range(HEADS):
                act.wait_ge(o_in[k % 2], i0 + 16 * (k // 2 + 1))
                act.activation(g.Hh[:, k, :], b.o[:, k % 2, :], ACT.Copy).then_inc(b.o_hi, 1)
            for m in range(2, KC):
                act.wait_ge(b.w_lo, k0 + m - 1)
                w_load(m)
                w_hi(m)

        @block.gpsimd
        def _(pool):
            for m in range(KC):
                pool.wait_ge(b.w_hi, k0 + m + 1)
                pool.tensor_tensor(b.wl[:, m % 2, :, :], b.wr[:, m % 2, :, :], b.wh[:, m % 2, :, :].bitcast(F32),
                                   ALU.subtract).then_inc(b.w_lo, 1)

        @block.tensor
        def _(pe):
            pe.wait_ge(b.o_lo, k0 + HEADS)
            for m in range(KC):
                pe.wait_ge(b.w_lo, k0 + m + 1)
                for n in range(NN):
                    if m >= 2:
                        pe.wait_ge(b.added, b0 + 3 * (m - 2) + n + 1)
                    linear_bank(g, pe, 3 * (m % 2) + n, b.wh[:, m % 2], b.wl[:, m % 2], n).then_inc(b.mm, 1)

        @block.vector
        def _(dve):
            for k in range(HEADS):
                dve.wait_ge(b.o_hi, k0 + k + 1)
                dve.tensor_tensor(g.Hl[:, k, :], b.o[:, k % 2, :], g.Hh[:, k, :].bitcast(F32), ALU.subtract)\
                    .then_inc(b.o_lo, 1)
            dve.wait_ge(b.x_in, 16 * (layer + 1))
            for m in range(KC):
                for n in range(NN):
                    dve.wait_ge(b.mm, b0 + 3 * m + n + 1)
                    add_gated(g, dve, m, n, 3 * (m % 2) + n, gate).then_inc(b.added, 1)


def add_gated(g, dve, m, n, bank, gate):
    for lo, hi, cond in ((n * NB, min((n + 1) * NB, NS), 0), (max(n * NB, NS), (n + 1) * NB, 1)):
        if lo < hi:
            last = dve.scalar_tensor_tensor(g.x[:, m, lo:hi], g.PS[:, bank, lo - n * NB:hi - n * NB],
                                            g.mod[:, gate + m, cond:cond + 1], g.x[:, m, lo:hi], ALU.mult, ALU.add)
    return last


def phase_ffn(g, layer):
    nc, PS = g.nc, g.PS
    w_up, w_down = chunks(g.a.w_up[layer]), chunks(g.a.w_down[layer])
    gate = NMOD * layer + G_F
    b, stack = scope(g, f"ff{layer}", {
        "wr": ([P, 2, KC, P], F32), "wh": ([P, 2, KC, P], F32R), "wl": ([P, 2, KC, P], F32R),
        "dr": ([P, 2, D], F32), "dh": ([P, 2, D], F32R), "dl": ([P, 2, D], F32R),
        "u": ([P, 2, PADT + 2], F32), "c": ([P, 4, PADT], F32),
        "ah": ([P, 2, T], F32R), "al": ([P, 2, T], F32R)},
        "pads w_in0 w_in1 d_in w_hi w_lo d_hi d_lo up_mm up_out conv silu prod a_hi a_lo dn_mm dn_add")
    w_in = [b.w_in0, b.w_in1]
    DN = KC * NN

    def groups(eng, body):
        body(0, first=True, last=False)
        body(1, first=False, last=False)
        with eng.Fori(2, GROUPS - 1) as i:
            body(i, first=False, last=False)
        body(GROUPS - 1, first=False, last=True)

    with stack, nc.Block() as block:
        @block.sync
        def _(sp):
            def load(i, j):
                col = (j % 2) * FC + 2 * i + j // 2
                sp.dma_start(b.wr[:, j % 2, :, :], w_up[:, :, bass.ds(col * P, P)]).then_inc(w_in[j % 2], 16)

            load(0, 0)
            load(0, 1)

            def body(i, first, last):
                for j in range(4):
                    if j == 2:
                        if not first:
                            sp.wait_ge(b.d_lo, i)
                        sp.dma_start(b.dr[:, :, :], w_down[:, bass.ds(2 * i, 2), :]).then_inc(b.d_in, 16)
                    if last and j >= 2:
                        continue
                    sp.wait_ge(b.w_lo, 4 * i + j + 1)
                    if j < 2:
                        load(i, j + 2)
                    else:
                        load(i + 1, j - 2)
            groups(sp, body)

        @block.scalar
        def _(act):
            def w_hi(i, j, fresh=False):
                act.wait_ge(w_in[j % 2], 16 * (2 * i + j // 2 + 1))
                if not fresh:
                    act.wait_ge(b.up_mm, 4 * i + j - 1)
                act.activation(b.wh[:, j % 2, :, :], b.wr[:, j % 2, :, :], ACT.Copy).then_inc(b.w_hi, 1)

            act.wait_ge(b.pads, 1)
            w_hi(0, 0, fresh=True)
            w_hi(0, 1, fresh=True)

            def body(i, first, last):
                for j in range(4):
                    act.wait_ge(b.up_mm, 4 * i + j + 1)
                    if not (first and j < 2):
                        act.wait_ge(b.conv, 3 * (4 * i + j - 1))
                    s, u = 3 * (j % 2), b.u[:, j % 2, :]
                    act.activation(u[:, 1:1 + 2 * NB].rearrange("p (n t) -> p n t", n=2), PS[:, s:s + 2, 0:NB], ACT.Copy)
                    act.activation(u[:, 1 + 2 * NB:1 + NS], PS[:, s + 2, 0:NS - 2 * NB], ACT.Copy)
                    act.activation(u[:, 2 + NS:2 + NS + NP], PS[:, s + 2, NS - 2 * NB:NB], ACT.Copy).then_inc(b.up_out, 1)
                    if not (last and j >= 2):
                        w_hi(i + (j + 2) // 4, (j + 2) % 4)
                    if j % 2:
                        q = 2 * i + j // 2
                        act.wait_ge(b.conv, 3 * (4 * i + j))
                        act.activation(b.c[:, j - 1, :], b.c[:, j - 1, :], ACT.Silu).then_inc(b.silu, 1)
                        act.wait_ge(b.prod, q + 1)
                        if j == 1 and not first:
                            act.wait_ge(b.dn_mm, DN * i)
                        act.activation(b.ah[:, j // 2, 0:NS], b.c[:, j, 0:NS], ACT.Copy)
                        act.activation(b.ah[:, j // 2, NS:T], b.c[:, j, NS + 1:PADT], ACT.Copy).then_inc(b.a_hi, 1)
                    if j == 1:
                        act.wait_ge(b.d_in, 16 * (i + 1))
                        act.activation(b.dh[:, :, :], b.dr[:, :, :], ACT.Copy).then_inc(b.d_hi, 1)
            groups(act, body)

        @block.gpsimd
        def _(pool):
            for s in range(2):
                for c in (0, NS + 1, NS + NP + 2):
                    last = pool.memset(b.u[:, s, c:c + 1], 0.0)
            last.then_inc(b.pads, 1)

            def w_lo(i, j):
                pool.wait_ge(b.w_hi, 4 * i + j + 1)
                pool.tensor_tensor(b.wl[:, j % 2, :, :], b.wr[:, j % 2, :, :], b.wh[:, j % 2, :, :].bitcast(F32),
                                   ALU.subtract).then_inc(b.w_lo, 1)

            w_lo(0, 0)
            w_lo(0, 1)

            def body(i, first, last):
                for j in range(4):
                    if not (last and j >= 2):
                        w_lo(i + (j + 2) // 4, (j + 2) % 4)
                    if j % 2:
                        pool.wait_ge(b.a_hi, 2 * i + j // 2 + 1)
                        pool.tensor_tensor(b.al[:, j // 2, 0:NS], b.c[:, j, 0:NS], b.ah[:, j // 2, 0:NS].bitcast(F32),
                                           ALU.subtract)
                        pool.tensor_tensor(b.al[:, j // 2, NS:T], b.c[:, j, NS + 1:PADT],
                                           b.ah[:, j // 2, NS:T].bitcast(F32), ALU.subtract).then_inc(b.a_lo, 1)
                    if j == 1:
                        pool.wait_ge(b.d_hi, i + 1)
                        pool.tensor_tensor(b.dl[:, :, :], b.dr[:, :, :], b.dh[:, :, :].bitcast(F32),
                                           ALU.subtract).then_inc(b.d_lo, 1)
            groups(pool, body)

        @block.tensor
        def _(pe):
            def up(i, j, first):
                pe.wait_ge(b.w_lo, 4 * i + j + 1)
                if not (first and j < 2):
                    pe.wait_ge(b.up_out, 4 * i + j - 1)
                for n in range(NN):
                    last = linear_bank(g, pe, 3 * (j % 2) + n, b.wh[:, j % 2], b.wl[:, j % 2], n)
                last.then_inc(b.up_mm, 1)

            def down(i, fresh):
                pe.wait_ge(b.a_lo, 2 * i + 2)
                pe.wait_ge(b.d_lo, i + 1)
                for m in range(KC):
                    for n in range(NN):
                        x = m * NN + n
                        if not (fresh and x < 2):
                            pe.wait_ge(b.dn_add, DN * i + x - 1)
                        for k in range(2):
                            last = product(pe, PS[:, 6 + x % 2, 0:NB], b.dh[:, k, m * P:(m + 1) * P],
                                           b.dl[:, k, m * P:(m + 1) * P], b.ah[:, k, n * NB:(n + 1) * NB],
                                           b.al[:, k, n * NB:(n + 1) * NB], k == 0, k == 1)
                        last.then_inc(b.dn_mm, 1)

            def body(i, first, last):
                up(i, 0, first)
                up(i, 1, first)
                if not first:
                    down(i - 1, fresh=isinstance(i, int) and i == 1)
                up(i, 2, first)
                up(i, 3, first)

            groups(pe, body)
            down(GROUPS - 1, fresh=False)

        @block.vector
        def _(dve):
            def conv(i, j, step):
                n = 3 * (4 * i + j)
                tap = lambda t: g.par[:, bass.ds(col + t * 2 * FC, 1)]
                col = PC_CW + layer * 3 * 2 * FC + (j % 2) * FC + 2 * i + j // 2
                bias = g.par[:, bass.ds(PC_CB + layer * 2 * FC + (j % 2) * FC + 2 * i + j // 2, 1)]
                c, u = b.c[:, j, :], b.u[:, j % 2, :]
                if step == 0:
                    dve.wait_ge(b.up_out, 4 * i + j + 1)
                    dve.tensor_scalar(c, u[:, 0:PADT], tap(0), bias, ALU.mult, ALU.add).then_inc(b.conv, 1)
                else:
                    dve.wait_ge(b.conv, n + step)
                    dve.scalar_tensor_tensor(c, u[:, step:step + PADT], tap(step), c, ALU.mult, ALU.add).then_inc(b.conv, 1)

            def mult(i, j):
                dve.wait_ge(b.conv, 3 * (4 * i + j) + 3)
                dve.wait_ge(b.silu, 2 * i + j // 2 + 1)
                dve.tensor_tensor(b.c[:, j, :], b.c[:, j - 1, :], b.c[:, j, :], ALU.mult).then_inc(b.prod, 1)

            def add_bank(i, x, fresh):
                dve.wait_ge(b.dn_mm, DN * i + x + 1)
                if x == 0 and not fresh:
                    dve.wait_ge(b.dn_add, DN * i)
                add_gated(g, dve, x // NN, x % NN, 6 + x % 2, gate).then_inc(b.dn_add, 1)

            def body(i, first, last):
                if not first:
                    dve.wait_ge(b.a_lo, 2 * i)
                for s in range(3):
                    conv(i, 0, s)
                if first:
                    for s in range(3):
                        conv(i, 1, s)
                    mult(i, 1)
                else:
                    for x in range(DN):
                        add_bank(i - 1, x, isinstance(i, int) and i == 1)
                        if x in (1, 3, 5):
                            conv(i, 1, (x - 1) // 2)
                        if x == 7:
                            mult(i, 1)
                for j in (2, 3):
                    for s in range(3):
                        conv(i, j, s)
                mult(i, 3)
            groups(dve, body)
            for x in range(DN):
                add_bank(GROUPS - 1, x, False)


def phase_final(g):
    nc, a, PS = g.nc, g.a, g.PS
    b, stack = scope(g, "fin", {
        "w": ([P, D], F32), "sq": ([P, D], F32), "ss": ([P, TT], F32), "ms": ([P, TT], F32), "r": ([P, TT], F32),
        "y": ([P, 2, D], F32)}, "w_in xt sq_d ms_d r_d y_d y_out0 y_out1")
    y_out = [b.y_out0, b.y_out1]
    with stack, nc.Block() as block:
        @block.tensor
        def _(pe):
            for t in range(TT):
                if t >= 4:
                    pe.wait_ge(b.y_d, t - 3)
                for k in range(KC):
                    last = pe.transpose(PS[:, 2 * (t % 4) + k // 4, (k % 4) * P:(k % 4 + 1) * P],
                                        g.x[:, k, t * P:(t + 1) * P], g.ident[:, :])
                last.then_inc(b.xt, 1)

        tile = lambda t: PS[:, 2 * (t % 4):2 * (t % 4) + 2, :]
        two = lambda ap: ap.rearrange("p (n c) -> p n c", n=2)

        @block.scalar
        def _(act):
            act.dma_start(b.w[:, :], a.final_norm.partition_broadcast(P)).then_inc(b.w_in, 16)
            for t in range(TT):
                act.wait_ge(b.xt, t + 1)
                if t:
                    act.wait_ge(b.sq_d, t)
                act.activation(two(b.sq[:, :]), tile(t), ACT.Square, accum_out=b.ss[:, t:t + 1]).then_inc(b.sq_d, 1)

        @block.gpsimd
        def _(pool):
            for t in range(TT):
                pool.wait_ge(b.ms_d, t + 1)
                pool.tensor_tensor(b.r[:, t:t + 1], b.ms[:, t:t + 1], g.half[:, 0:1], ALU.pow).then_inc(b.r_d, 1)

        @block.vector
        def _(dve):
            dve.wait_ge(b.w_in, 16)

            def mean(t):
                dve.wait_ge(b.sq_d, t + 1)
                dve.tensor_scalar(b.ms[:, t:t + 1], b.ss[:, t:t + 1], 1.0 / D, EPS, ALU.mult, ALU.add).then_inc(b.ms_d, 1)

            mean(0)
            for t in range(TT):
                if t + 1 < TT:
                    mean(t + 1)
                dve.wait_ge(b.r_d, t + 1)
                if t >= 2:
                    dve.wait_ge(y_out[t % 2], 16 * (t // 2))
                dve.scalar_tensor_tensor(two(b.y[:, t % 2, :]), tile(t), b.r[:, t:t + 1], two(b.w[:, :]), ALU.mult,
                                         ALU.mult).then_inc(b.y_d, 1)

        @block.sync
        def _(sp):
            for t in range(TT):
                sp.wait_ge(b.y_d, t + 1)
                dst = a.y_sample[0, t * P:(t + 1) * P, :] if t < QT else a.y_prompt[0, :, :]
                sp.dma_start(dst, b.y[:, t % 2, :]).then_inc(y_out[t % 2], 16)
            sp.wait_ge(b.y_out0, 16 * 5)
            sp.wait_ge(b.y_out1, 16 * 4)


def rope_swap(eng, dst, src, sem):
    for blk in range(4):
        for half in range(2):
            to, of = 32 * blk + 16 * half, 32 * blk + 16 * (1 - half)
            eng.dma_start(dst[to:to + 16, :], src[of:of + 16, :]).then_inc(sem, 16)


SWAP = 16 * 8
STACK = 16 * 4


def stack_keys(eng, dst, b, sem):
    for m in range(2):
        for half, src in ((0, b.nkh), (1, b.nkl)):
            eng.dma_start(dst[half * DH:(half + 1) * DH, m, :].bitcast(F32), src[m * DH:(m + 1) * DH, :].bitcast(F32)).then_inc(sem, 16)


def stack_queries(eng, b, sem):
    for dst, src in ((b.qsh, b.nqh), (b.qsl, b.nql)):
        for m in range(2):
            for half in range(2):
                eng.dma_start(dst[half * DH:(half + 1) * DH, m, :].bitcast(F32), src[m * DH:(m + 1) * DH, :].bitcast(F32)).then_inc(sem, 16)


def rotate_and_split(link, dve, x, lo_part, hi_part, off, width, cos, sin):
    s = slice(off, off + NS)
    link(dve.tensor_tensor(x[:, s], x[:, s], cos[:, :], ALU.mult))
    link(dve.tensor_tensor(lo_part[:, s].bitcast(F32), lo_part[:, s].bitcast(F32), sin[:, :], ALU.mult))
    link(dve.tensor_tensor(x[:, s], x[:, s], lo_part[:, s].bitcast(F32), ALU.add))
    link(dve.tensor_copy(hi_part[:, 0:width], x[:, 0:width]))
    link(dve.tensor_tensor(lo_part[:, 0:width], x[:, 0:width], hi_part[:, 0:width].bitcast(F32), ALU.subtract))


ROPE_STEPS = 5


def scores(g, pe, b, m, t):
    spans = [(n, n * NB, NB) for n in range(NN)] if t < QT else [(0, NKEY, P)]
    for n, key, width in spans:
        for q in (b.qsh, b.qsl):
            last = pe.matmul(g.PS[:, 3 * m + n, 0:width], q[:, m, t * P:(t + 1) * P], b.ks[:, m, key:key + width],
                             start=q is b.qsh, stop=q is b.qsl)
    return last


def banks(g, m, t):
    return g.PS[:, 3 * m:3 * m + 3, 0:NB] if t < QT else g.PS[:, 3 * m, 0:P]


def like_banks(row, t):
    return row.rearrange("p (n t) -> p n t", n=NN) if t < QT else row[:, 0:P]


def keys(t):
    return NKEY if t < QT else P


TILES = QT + 1
STEPS = TILES + 1


def groups_of(t):
    return [(0, 3), (3, 3), (6, 3)] if t < QT else [(0, 1)]


PAIRS = [(0, 2), (2, 2), (4, 2), (6, 2), (8, 1)]


def transposes(g, pe, bank, row, c0, n):
    for c in range(n):
        last = pe.transpose(g.PS[:, bank, c * P:(c + 1) * P], row[:, (c0 + c) * P:(c0 + c + 1) * P], g.ident[:, :])
    return last


def value_chunk(t0, c):
    return c if t0 < QT else KW // P - 1


def phase_diff_attention(g):
    nc, a, PS = g.nc, g.a, g.PS
    w = chunks(a.w_qkv_diff[0])
    b, stack = scope(g, "da", {
        "wr": ([P, KC, P], F32), "wh": ([P, 2, KC, P], F32R), "wl": ([P, 2, KC, P], F32R),
        "cos": ([P, NS], F32), "sin": ([P, NS], F32),
        "q": ([P, T], F32), "k": ([P, KW], F32), "vt": ([P, T], F32),
        "nqh": ([P, T], F32R), "nql": ([P, T], F32R), "nkh": ([P, KW], F32R), "nkl": ([P, KW], F32R),
        "qsh": ([P, 2, T], F32R), "qsl": ([P, 2, T], F32R), "ks": ([P, 2, KW], F32R),
        "v": ([P, KW // P, P], F32), "e0": ([P, 2, NKEY], F32), "e1": ([P, NKEY], F32),
        "pt": ([P, TT, 2 * P], F32), "o": ([P, 2 * P], F32), "sq": ([P, 2 * P], F32), "y": ([P, 2 * P], F32),
        "ck": ([P, P], F32), "ko": ([P, P], F32),
        "mx": ([P, 2], F32), "nb": ([P, 2], F32), "l": ([P, 2], F32), "rl": ([P, 2], F32), "c2": ([P, 1], F32),
        "ms": ([P, 2], F32), "r": ([P, 2], F32), "wsub": ([P, 1], F32)},
        "tab w_in w_hi w_lo free0 free1 full s_mm nmax exp prob rope kswap qswap kst qst"
        " ck_in cv_in ko_out v_out r_d y_out sub soft")
    free = {WORK: b.free0, WORK + 1: b.free1}

    def step_uses(s, ahead):
        pair = {2: 0, 4: 1, 6: 2, 8: 3}
        norm = {3: 0, 5: 1, 7: 2, 9: 3}
        proj = {0: ("k", 0), 1: ("k", 1), 2: ("k", 2), 3: ("q", 0), 4: ("q", 1), 5: ("q", 2), 9: ("v", 0)}
        u = [("vt", i) for i in range(3)] if s == 0 else [("T", s - 1, i) for i in range(len(groups_of(s - 1)))]
        u += [("PV", pair[s])] if s in pair else []
        u += [("ST", norm[s])] if s in norm else []
        if ahead and s in proj:
            u += [("W",) + proj[s]]
        if ahead and s in (2, 3):
            u += [("ck",) if s == 2 else ("ko",)]
        u += [("BC", norm[s])] if s in norm else []
        if s == STEPS - 1:
            u += [("PV", 4)] + [("W", "v", 1)] * ahead + [("ST", 4)] + [("W", "v", 2)] * ahead + [("BC", 4)]
        return u

    FIRST = [("W", "k", 0), ("W", "k", 1), ("W", "k", 2), ("ck",), ("ko",), ("W", "q", 0), ("W", "q", 1), ("W", "q", 2),
             ("W", "v", 0), ("W", "v", 1), ("W", "v", 2)]
    BODY = [u for s in range(STEPS) for u in step_uses(s, True)]
    LAST = [u for s in range(STEPS) for u in step_uses(s, False)]
    assert len(BODY) % 2 == 0
    AFTER_PV = len(BODY) - BODY.index(("PV", 4)) - 1
    UNIT = {"k": 0, "q": 1, "v": 2}
    SLOT = {"k": 1, "q": 0, "v": 0}
    COL = {"q": 0, "k": HEADS, "v": 2 * HEADS}

    def heads(eng, first, body):
        first(Ring(0, 0, FIRST, None))
        with eng.Fori(0, HEADS - 1) as h:
            body(h, Ring(len(FIRST), len(BODY), BODY, h), True)
        body(HEADS - 1, Ring(len(FIRST) + (HEADS - 1) * len(BODY), 0, LAST, 0), False)

    with stack, nc.Block() as block:
        @block.sync
        def _(sp):
            def load_w(h, x):
                if not (isinstance(h, int) and h == 0 and x == "k"):
                    sp.wait_ge(b.w_lo, 3 * h + UNIT[x])
                sp.dma_start(b.wr[:, :, :], w[:, :, bass.ds((COL[x] + h) * P, P)]).then_inc(b.w_in, 16)

            def one(ap, h):
                return ap[0, 0, bass.ds(h, 1)].rearrange("o s d -> (o s) d")

            def cached_keys(h):
                sp.dma_start(b.ck[:, :], one(a.cache_k_diff, h)).then_inc(b.ck_in, 16)

            def new_keys(h, ring):
                ring.wait_read(sp, free, ("ko",))
                sp.dma_start(one(a.new_k_diff, h), b.ko[:, :]).then_inc(b.ko_out, 16)

            def swap_keys(h, ring, fresh):
                if not fresh:
                    sp.wait_ge(b.kst, STACK * h)
                wait_both(sp, ring.read(free, ("W", "k", 1)), ring.read(free, ("W", "k", 2)))
                rope_swap(sp, b.nkl[:, PAST:NKEY].bitcast(F32), b.k[:, PAST:NKEY], b.kswap)

            def swap_queries(h, ring, fresh):
                if not fresh:
                    sp.wait_ge(b.qst, 2 * STACK * h)
                wait_both(sp, ring.read(free, ("W", "q", 1)), ring.read(free, ("W", "q", 2)))
                rope_swap(sp, b.nql[:, 0:NS].bitcast(F32), b.q[:, 0:NS], b.qswap)

            def stacks(h, fresh):
                if not fresh:
                    sp.wait_ge(b.s_mm, 2 * TILES * h)
                sp.wait_ge(b.rope, 2 * ROPE_STEPS * h + ROPE_STEPS)
                stack_keys(sp, b.ks, b, b.kst)
                sp.wait_ge(b.rope, 2 * ROPE_STEPS * h + 2 * ROPE_STEPS)
                stack_queries(sp, b, b.qst)

            def first(ring):
                load_w(0, "k")
                cached_keys(0)
                sp.dma_start(b.cos[:, :], a.rope_cos).then_inc(b.tab, 16)
                load_w(0, "q")
                swap_keys(0, ring, True)
                load_w(0, "v")
                new_keys(0, ring)
                swap_queries(0, ring, True)
                stacks(0, True)

            def body(h, ring, ahead):
                if ahead:
                    load_w(h + 1, "k")
                    cached_keys(h + 1)
                wait_both(sp, (b.full, ring.before + ring.index * ring.per_head - AFTER_PV), (b.v_out, 16 * h + 16))
                sp.dma_start(b.v[:, 0, :], one(a.cache_v_diff, h)).then_inc(b.cv_in, 16)
                if ahead:
                    load_w(h + 1, "q")
                ring.wait_read(sp, free, ("vt", 2))
                sp.dma_start(one(a.new_v_diff, h), b.v[:, KW // P - 1, :]).then_inc(b.v_out, 16)
                if ahead:
                    swap_keys(h + 1, ring, False)
                    new_keys(h + 1, ring)
                    load_w(h + 1, "v")
                    swap_queries(h + 1, ring, False)
                    stacks(h + 1, False)

            heads(sp, first, body)
            sp.wait_ge(b.ko_out, 16 * HEADS)
            sp.wait_ge(b.v_out, 16 * HEADS + 16)

        @block.scalar
        def _(act):
            def w_hi(h, x):
                n = 3 * h + UNIT[x]
                act.wait_ge(b.w_in, 16 * n + 16)
                act.activation(b.wh[:, SLOT[x], :, :], b.wr[:, :, :], ACT.Copy).then_inc(b.w_hi, 1)

            def copy_out(ring, use, dst, cols, parts=1):
                act.wait_ge(b.full, ring.done(use))
                src = PS[:, ring.bank(use), 0:cols]
                act.activation(dst, src.rearrange("p (n t) -> p n t", n=parts) if parts > 1 else src, ACT.Copy)\
                    .then_inc(free[ring.bank(use)], 1)

            def project(ring, x, n):
                dst, off = {"k": (b.k, PAST), "q": (b.q, 0), "v": (b.vt, 0)}[x]
                copy_out(ring, ("W", x, n), dst[:, off + n * NB:off + (n + 1) * NB], NB)

            def softmax(h, t):
                for m in range(2):
                    e = b.e0[:, t % 2, :] if m == 0 else b.e1[:, :]
                    act.wait_ge(b.nmax, 2 * (TILES * h + t) + m + 1)
                    act.activation(like_banks(e, t), banks(g, m, t), ACT.Exp, bias=b.nb[:, m:m + 1], scale=SCALE,
                                   accum_out=b.l[:, m:m + 1]).then_inc(b.exp, 1)

            def outputs(ring, h, p):
                n = PAIRS[p][1] * P
                if p:
                    ring.wait_read(act, free, ("BC", p - 1))
                act.wait_ge(b.full, ring.done(("PV", p)))
                act.activation(b.sq[:, 0:n], PS[:, ring.bank(("PV", p)), 0:n], ACT.Square)
                copy_out(ring, ("PV", p), b.o[:, 0:n], n)

            def first(ring):
                w_hi(0, "k")
                for x in FIRST:
                    if x[0] == "W":
                        if x[1:] == ("k", 2):
                            w_hi(0, "q")
                        if x[1:] == ("q", 2):
                            project(ring, *x[1:])
                            w_hi(0, "v")
                            continue
                        project(ring, *x[1:])
                    elif x[0] == "ck":
                        copy_out(ring, x, b.k[:, 0:PAST], P)
                    else:
                        copy_out(ring, x, b.ko[:, :], P)

            def body(h, ring, ahead):
                for s in range(STEPS):
                    if s == 0 and ahead:
                        w_hi(h + 1, "k")
                    if s == 2 and ahead:
                        w_hi(h + 1, "q")
                    for use in step_uses(s, ahead):
                        if use[0] == "vt":
                            if use[1] == 0:
                                act.wait_ge(b.v_out, 16 * h + 16)
                            copy_out(ring, use, b.v[:, 1 + 3 * use[1]:4 + 3 * use[1], :], NB, 3)
                        if use[0] == "T":
                            t, (c0, n) = use[1], groups_of(use[1])[use[2]]
                            dst = b.pt[:, c0:c0 + n, (t % 2) * P:(t % 2 + 1) * P]
                            copy_out(ring, use, dst if n > 1 else dst[:, 0, :], n * P, n)
                    if s < TILES:
                        softmax(h, s)
                    for use in step_uses(s, ahead):
                        if use[0] == "PV":
                            outputs(ring, h, use[1])
                        if use[0] == "W":
                            project(ring, *use[1:])
                        if use[0] == "ck":
                            copy_out(ring, use, b.k[:, 0:PAST], P)
                        if use[0] == "ko":
                            act.wait_ge(b.ko_out, 16 * h + 16)
                            copy_out(ring, use, b.ko[:, :], P)
                    if s == 5 and ahead:
                        w_hi(h + 1, "v")

            heads(act, first, body)

        @block.gpsimd
        def _(pool):
            def w_lo(h, x):
                n = 3 * h + UNIT[x]
                pool.wait_ge(b.w_hi, n + 1)
                pool.tensor_tensor(b.wl[:, SLOT[x], :, :], b.wr[:, :, :], b.wh[:, SLOT[x], :, :].bitcast(F32), ALU.subtract)\
                    .then_inc(b.w_lo, 1)

            def root(ring, p):
                n = PAIRS[p][1]
                ring.wait_read(pool, free, ("ST", p))
                pool.tensor_tensor(b.r[:, 0:n], b.ms[:, 0:n], g.half[:, 0:n], ALU.pow).then_inc(b.r_d, 1)

            def store(ring, h, p):
                t0, n = PAIRS[p]
                ring.wait_read(pool, free, ("BC", p))
                pool.dma_start(g.o_save[bass.ds(h, 1), :, t0 * P:(t0 + n) * P].rearrange("o p t -> (o p) t"), b.y[:, 0:n * P])\
                    .then_inc(b.y_out, 16)

            def first(ring):
                pool.memset(b.v[:, KW // P - 1, :], 0.0).then_inc(b.v_out, 16)
                pool.dma_start(b.sin[:, :], a.rope_sin).then_inc(b.y_out, 16)
                for x in "kqv":
                    w_lo(0, x)

            def body(h, ring, ahead):
                for s in range(STEPS):
                    if ahead and s in (0, 2, 5):
                        w_lo(h + 1, {0: "k", 2: "q", 5: "v"}[s])
                    for use in step_uses(s, ahead):
                        if use[0] == "ST":
                            root(ring, use[1])
                        if use[0] == "BC":
                            store(ring, h, use[1])

            heads(pool, first, body)
            pool.wait_ge(b.y_out, 16 * len(PAIRS) * HEADS + 16)

        @block.tensor
        def _(pe):
            def project(ring, h, x, n):
                if n == 0:
                    pe.wait_ge(b.w_lo, 3 * h + UNIT[x] + 1)
                ring.wait_free(pe, free, ("W", x, n))
                last = linear_bank(g, pe, ring.bank(("W", x, n)), b.wh[:, SLOT[x]], b.wl[:, SLOT[x]], n)
                last.then_inc(b.full, 1)

            def do(ring, h, use):
                what, bank = use[0], ring.bank(use)
                if what == "W":
                    return project(ring, h + 1 if ring.head is not None else 0, *use[1:])
                ring.wait_free(pe, free, use)
                out = PS[:, bank, :]
                if what == "vt":
                    for c in range(3):
                        t = 3 * use[1] + c
                        last = pe.transpose(out[:, c * P:(c + 1) * P], b.vt[:, t * P:(t + 1) * P], g.ident[:, :])
                elif what == "ck":
                    pe.wait_ge(b.ck_in, 16 * (h + 1) + 16 if ring.head is not None else 16)
                    last = pe.transpose(out[:, 0:P], b.ck[:, :], g.ident[:, :])
                elif what == "ko":
                    ring.wait_read(pe, free, ("W", "k", 2))
                    last = pe.transpose(out[:, 0:P], b.k[:, NKEY:KW], g.ident[:, :])
                elif what == "T":
                    t, (c0, n) = use[1], groups_of(use[1])[use[2]]
                    if use[2] == 0:
                        pe.wait_ge(b.prob, TILES * h + t + 1)
                    last = transposes(g, pe, bank, b.e0[:, t % 2, :], c0, n)
                elif what == "PV":
                    t0, n = PAIRS[use[1]]
                    if use[1] == 0:
                        pe.wait_ge(b.cv_in, 16 * h + 16)
                    for t in (t0, t0 + n - 1):
                        for i in range(len(groups_of(t)))[-2:]:
                            ring.wait_read(pe, free, ("T", t, i))
                    nk = keys(t0) // P
                    for c in range(nk):
                        last = pe.matmul(out[:, 0:n * P], b.v[:, value_chunk(t0, c), :], b.pt[:, c, 0:n * P],
                                         start=c == 0, stop=c == nk - 1)
                elif what == "ST":
                    ring.wait_read(pe, free, ("PV", use[1]))
                    for i in range(PAIRS[use[1]][1]):
                        last = pe.matmul(out[:, i:i + 1], b.sq[:, i * P:(i + 1) * P], g.ones_v[:, :], start=True, stop=True)
                elif what == "BC":
                    pe.wait_ge(b.r_d, len(PAIRS) * h + use[1] + 1)
                    for i in range(PAIRS[use[1]][1]):
                        last = pe.matmul(out[:, i * P:(i + 1) * P], b.r[:, i:i + 1].to_broadcast([P, P]), g.ident[:, :],
                                         start=True, stop=True)
                last.then_inc(b.full, 1)

            def first(ring):
                for use in FIRST:
                    do(ring, 0, use)

            def body(h, ring, ahead):
                for s in range(STEPS):
                    if s == 0:
                        pe.wait_ge(b.kst, STACK * h + STACK)
                        pe.wait_ge(b.qst, 2 * STACK * h + 2 * STACK)
                    for m in range(2):
                        if s < TILES:
                            if s:
                                pe.wait_ge(b.exp, 2 * (TILES * h + s) + m - 1)
                            scores(g, pe, b, m, s).then_inc(b.s_mm, 1)
                    for use in step_uses(s, ahead):
                        do(ring, h, use)

            heads(pe, first, body)

        @block.vector
        def _(dve):
            def rope(h, x):
                n = 2 * ROPE_STEPS * h + (ROPE_STEPS if x == "q" else 0)
                link = Chain(dve, b.rope, n)
                if x == "k":
                    dve.wait_ge(b.kswap, SWAP * h + SWAP)
                    rotate_and_split(link, dve, b.k, b.nkl, b.nkh, PAST, KW, b.cos, b.sin)
                else:
                    dve.wait_ge(b.qswap, SWAP * h + SWAP)
                    rotate_and_split(link, dve, b.q, b.nql, b.nqh, 0, T, b.cos, b.sin)

            dve.wait_ge(b.tab, 16)
            dve.wait_ge(b.y_out, 16)
            dve.tensor_scalar(b.wsub[:, :], g.par[:, PC_SUB:PC_SUB + 1], 1.0 - LAMBDA_INIT, None, ALU.mult).then_inc(b.sub, 1)
            dve.wait_ge(b.sub, 1)

            def first(ring):
                ring.wait_read(dve, free, ("ck",))
                ring.wait_read(dve, free, ("ko",))
                rope(0, "k")
                rope(0, "q")

            SOFT = 5

            def body(h, ring, ahead):
                for s in range(STEPS):
                    if s < TILES:
                        link = Chain(dve, b.soft, SOFT * (TILES * h + s))
                        for m in range(2):
                            dve.wait_ge(b.s_mm, 2 * (TILES * h + s) + m + 1)
                            link(dve.reduce_max(b.mx[:, m:m + 1], banks(g, m, s), AX.XY if s < QT else AX.X))
                            dve.tensor_scalar(b.nb[:, m:m + 1], b.mx[:, m:m + 1], -SCALE, None, ALU.mult).then_inc(b.nmax, 1)
                    uses = step_uses(s, ahead)
                    mean = [u for u in uses if u[0] == "ST"]
                    scale = [u for u in uses if u[0] == "BC"]

                    def mean_square(use):
                        n = PAIRS[use[1]][1]
                        dve.wait_ge(b.full, ring.done(use))
                        dve.tensor_scalar(b.ms[:, 0:n], PS[:, ring.bank(use), 0:n], EPS, None, ALU.add)\
                            .then_inc(free[ring.bank(use)], 1)

                    def normalise(use):
                        n = PAIRS[use[1]][1] * P
                        dve.wait_ge(b.full, ring.done(use))
                        dve.wait_ge(b.y_out, 16 * (len(PAIRS) * h + use[1] + 1))
                        dve.scalar_tensor_tensor(b.y[:, 0:n], b.o[:, 0:n], b.wsub[:, :], PS[:, ring.bank(use), 0:n],
                                                 ALU.mult, ALU.mult).then_inc(free[ring.bank(use)], 1)

                    if mean:
                        mean_square(mean[0])
                    if s < TILES:
                        e0, e1 = b.e0[:, s % 2, 0:keys(s)], b.e1[:, 0:keys(s)]
                        dve.wait_ge(b.exp, 2 * (TILES * h + s) + 2)
                        link(dve.reciprocal(b.rl[:, :], b.l[:, :]))
                        link(dve.tensor_scalar(b.c2[:, :], b.rl[:, 1:2], g.lam[:, 0:1], None, ALU.mult))
                        link(dve.tensor_scalar(e0, e0, b.rl[:, 0:1], None, ALU.mult))
                        dve.scalar_tensor_tensor(e0, e1, b.c2[:, :], e0, ALU.mult, ALU.add).then_inc(b.prob, 1)
                    if scale:
                        normalise(scale[0])
                    if s == STEPS - 1:
                        mean_square(mean[1])
                        normalise(scale[1])
                    if ahead and s == 4:
                        ring.wait_read(dve, free, ("ck",))
                        ring.wait_read(dve, free, ("ko",))
                        rope(h + 1, "k")
                    if ahead and s == 7:
                        rope(h + 1, "q")

            heads(dve, first, body)


def gqa_columns(ap, p):
    return ap[:, :, D + p * P:D + (p + 1) * P]


def phase_gqa_keys(g):
    nc, a, PS = g.nc, g.a, g.PS
    w = chunks(a.w_qkv_gqa[0])
    b, stack = scope(g, "gk", {
        "wr": ([P, 2, KC, P], F32), "wh": ([P, 2, KC, P], F32R), "wl": ([P, 2, KC, P], F32R),
        "cos": ([P, NS], F32), "sin": ([P, NS], F32), "k": ([P, KW], F32), "vt": ([P, T], F32), "sq": ([P, T], F32),
        "nkh": ([P, KW], F32R), "nkl": ([P, KW], F32R), "v": ([P, KW // P, P], F32),
        "ck": ([P, P], F32), "ko": ([P, P], F32), "ms": ([P, TT, 2], F32), "r": ([P, TT, 2], F32)},
        "tab w_in0 w_in1 w_hi w_lo mm out ck_in cv_in kt k_d sq_d stat ms_d r_d bc normed ko_t ko_d kswap rope vt_t v_d saved")
    w_in = [b.w_in0, b.w_in1]
    with stack, nc.Block() as block:
        @block.sync
        def _(sp):
            def load(u):
                col = D + (u % 2) * 2 * P + (u // 2) * P
                sp.dma_start(b.wr[:, u % 2, :, :], w[:, :, col:col + P]).then_inc(w_in[u % 2], 16)

            load(0)
            load(1)
            sp.dma_start(b.cos[:, :], a.rope_cos).then_inc(b.tab, 16)
            sp.dma_start(b.sin[:, :], a.rope_sin).then_inc(b.tab, 16)
            for p in range(2):
                if p:
                    sp.wait_ge(b.saved, 16 * 9)
                for m in range(2):
                    sp.dma_start(b.ck[:, m * DH:(m + 1) * DH], a.cache_k_gqa[0, 0, 2 * p + m]).then_inc(b.ck_in, 16)
                    sp.dma_start(b.v[:, 0, m * DH:(m + 1) * DH], a.cache_v_gqa[0, 0, 2 * p + m]).then_inc(b.cv_in, 16)
                sp.wait_ge(b.normed, 3 * p + 3)
                rope_swap(sp, b.nkl[:, PAST:NKEY].bitcast(F32), b.k[:, PAST:NKEY], b.kswap)
                if p == 0:
                    for u in (2, 3):
                        sp.wait_ge(b.w_lo, u - 1)
                        load(u)
                sp.wait_ge(b.ko_d, p + 1)
                sp.wait_ge(b.v_d, 3 * p + 3)
                for m in range(2):
                    sp.dma_start(a.new_k_gqa[0, 0, 2 * p + m], b.ko[:, m * DH:(m + 1) * DH]).then_inc(b.saved, 16)
                    sp.dma_start(a.new_v_gqa[0, 0, 2 * p + m], b.v[:, KW // P - 1, m * DH:(m + 1) * DH]).then_inc(b.saved, 16)
                sp.wait_ge(b.cv_in, 32 * (p + 1))
                sp.dma_start(g.v_save[p], b.v[:, :, :].rearrange("p c d -> p (c d)")).then_inc(b.saved, 16)
                sp.wait_ge(b.rope, ROPE_STEPS * (p + 1))
                stack_keys(sp, g.k_save[p], b, b.saved)
            sp.wait_ge(b.saved, 16 * 18)

        @block.scalar
        def _(act):
            def w_hi(u):
                act.wait_ge(w_in[u % 2], 16 * (u // 2 + 1))
                act.activation(b.wh[:, u % 2, :, :], b.wr[:, u % 2, :, :], ACT.Copy).then_inc(b.w_hi, 1)

            w_hi(0)
            w_hi(1)
            for p in range(2):
                act.wait_ge(b.mm, 2 * p + 1)
                if p:
                    act.wait_ge(b.saved, 16 * 9)
                act.activation(b.k[:, PAST:KW].rearrange("p (n t) -> p n t", n=NN), PS[:, 0:3, 0:NB], ACT.Copy).then_inc(b.out, 1)
                act.wait_ge(b.out, 2 * p + 1)
                act.activation(b.sq[:, :], b.k[:, PAST:KW], ACT.Square).then_inc(b.sq_d, 1)
                act.wait_ge(b.kt, p + 1)
                act.activation(b.k[:, 0:PAST], PS[:, 6, 0:P], ACT.Copy).then_inc(b.k_d, 1)
                act.wait_ge(b.mm, 2 * p + 2)
                act.activation(b.vt[:, :].rearrange("p (n t) -> p n t", n=NN), PS[:, 3:6, 0:NB], ACT.Copy).then_inc(b.out, 1)
                if p == 0:
                    w_hi(2)
                    w_hi(3)
                act.wait_ge(b.ko_t, p + 1)
                act.activation(b.ko[:, :], PS[:, 7, 0:P], ACT.Copy).then_inc(b.ko_d, 1)
                for i in range(3):
                    act.wait_ge(b.vt_t, 3 * p + i + 1)
                    act.activation(b.v[:, 1 + 3 * i:4 + 3 * i, :], PS[:, 3 + i, 0:NB].rearrange("p (c d) -> p c d", c=3),
                                   ACT.Copy).then_inc(b.v_d, 1)

        @block.gpsimd
        def _(pool):
            for u in range(4):
                if u % 2 == 0 and u:
                    pool.wait_ge(b.ms_d, 1)
                pool.wait_ge(b.w_hi, u + 1)
                pool.tensor_tensor(b.wl[:, u % 2, :, :], b.wr[:, u % 2, :, :], b.wh[:, u % 2, :, :].bitcast(F32),
                                   ALU.subtract).then_inc(b.w_lo, 1)
                if u % 2:
                    p = u // 2
                    pool.wait_ge(b.ms_d, p + 1)
                    pool.tensor_tensor(b.r[:, :, :].rearrange("p a b -> p (a b)"), b.ms[:, :, :].rearrange("p a b -> p (a b)"),
                                       g.half[:, 0:1].to_broadcast([P, 2 * TT]), ALU.pow).then_inc(b.r_d, 1)

        @block.tensor
        def _(pe):
            for p in range(2):
                for x in range(2):
                    u = 2 * p + x
                    pe.wait_ge(b.w_lo, u + 1)
                    if p:
                        pe.wait_ge(*((b.normed, 3), (b.v_d, 3))[x])
                    for n in range(NN):
                        last = linear_bank(g, pe, 3 * x + n, b.wh[:, x], b.wl[:, x], n)
                    last.then_inc(b.mm, 1)
                    if x == 0:
                        pe.wait_ge(b.ck_in, 32 * (p + 1))
                        if p:
                            pe.wait_ge(b.k_d, p)
                        pe.transpose(PS[:, 6, 0:P], b.ck[:, :], g.ident[:, :]).then_inc(b.kt, 1)
                pe.wait_ge(b.sq_d, p + 1)
                if p:
                    pe.wait_ge(b.ko_d, 1)
                for t in range(TT):
                    last = pe.matmul(PS[:, 7, 2 * t:2 * t + 2], b.sq[:, t * P:(t + 1) * P], g.ones_h[:, :], start=True, stop=True)
                last.then_inc(b.stat, 1)
                pe.wait_ge(b.r_d, p + 1)
                for t in range(TT):
                    last = broadcast_heads(g, pe, PS[:, t // 3, (t % 3) * P:(t % 3 + 1) * P], b.r[:, t, :])
                last.then_inc(b.bc, 1)
                pe.wait_ge(b.normed, 3 * p + 3)
                pe.transpose(PS[:, 7, 0:P], b.k[:, NKEY:KW], g.ident[:, :]).then_inc(b.ko_t, 1)
                pe.wait_ge(b.out, 2 * p + 2)
                for i in range(3):
                    for c in range(3):
                        t = 3 * i + c
                        last = pe.transpose(PS[:, 3 + i, c * P:(c + 1) * P], b.vt[:, t * P:(t + 1) * P], g.ident[:, :])
                    last.then_inc(b.vt_t, 1)

        @block.vector
        def _(dve):
            dve.wait_ge(b.tab, 32)
            for p in range(2):
                dve.wait_ge(b.stat, p + 1)
                dve.tensor_scalar(b.ms[:, :, :].rearrange("p a b -> p (a b)"), PS[:, 7, 0:2 * TT], EPS, None, ALU.add).then_inc(b.ms_d, 1)
                dve.wait_ge(b.bc, p + 1)
                for n in range(NN):
                    s = slice(PAST + n * NB, PAST + (n + 1) * NB)
                    dve.scalar_tensor_tensor(b.k[:, s], b.k[:, s], g.par[:, PC_KN:PC_KN + 1], PS[:, n, 0:NB], ALU.mult,
                                             ALU.mult).then_inc(b.normed, 1)
                dve.wait_ge(b.normed, 3 * p + 3)
                dve.wait_ge(b.kswap, SWAP * (p + 1))
                dve.wait_ge(b.ko_t, p + 1)
                dve.wait_ge(b.k_d, p + 1)
                rotate_and_split(Chain(dve, b.rope, ROPE_STEPS * p), dve, b.k, b.nkl, b.nkh, PAST, KW, b.cos, b.sin)


def broadcast_heads(g, pe, out, r):
    for m in range(2):
        last = pe.matmul(out[m * DH:(m + 1) * DH, :], r[:, m:m + 1].to_broadcast([P, DH]), g.ident[:, :], start=True, stop=True)
    return last


def phase_gqa_attention(g):
    phase_gqa_keys(g)
    nc, a, PS = g.nc, g.a, g.PS
    w = chunks(a.w_qkv_gqa[0])
    b, stack = scope(g, "ga", {
        "wr": ([P, KC, 2, DH], F32), "wh": ([P, KC, P], F32R), "wl": ([P, KC, P], F32R),
        "cos": ([P, NS], F32), "sin": ([P, NS], F32), "q": ([P, T], F32),
        "nqh": ([P, T], F32R), "nql": ([P, T], F32R), "qsh": ([P, 2, T], F32R), "qsl": ([P, 2, T], F32R),
        "ks": ([P, 2, KW], F32R), "v": ([P, KW // P, P], F32), "e": ([P, 2, 2, NKEY], F32),
        "pt": ([P, 2, TT, 2 * P], F32), "y": ([P, 2 * P], F32),
        "mx": ([P, 2], F32), "nb": ([P, 2], F32), "l": ([P, 2], F32), "rl": ([P, 2], F32),
        "mark": ([P, 1], F32), "ms": ([P, TT, 2], F32), "r": ([P, TT, 2], F32)},
        "tab w_in w_hi w_lo free0 free1 full s_mm nmax exp rl_d prob rope qswap qst kv_in r_d y_out sq_d soft normed")
    free = {WORK: b.free0, WORK + 1: b.free1}
    sq = b.nql[:, :].bitcast(F32)

    def step_uses(s, ahead1, ahead2):
        pair = {2: 0, 4: 1, 6: 2, 8: 3, 9: 4}
        u = []
        if s >= 1:
            u += [("T", s - 1, m, i) for i in range(len(groups_of(s - 1))) for m in range(2)]
        if ahead1 and s == 1:
            u += [("QS",)]
        if ahead1 and s == 3:
            u += [("QB", 0), ("QB", 1), ("QB", 2)]
        u += [("PV", pair[s])] if s in pair else []
        if ahead2 and s == STEPS - 1:
            u += [("W", n) for n in range(NN)]
        return u

    def listed(ahead1, ahead2):
        return [u for s in range(STEPS) for u in step_uses(s, ahead1, ahead2)]

    FIRST = [("W", 0), ("W", 1), ("W", 2), ("QS",), ("QB", 0), ("QB", 1), ("QB", 2), ("V", 0), ("V", 1), ("V", 2)]
    BODY, NEXT, LAST = listed(True, True), listed(True, False), listed(False, False)
    assert len(BODY) % 2 == 0

    def chunks_of_q(eng, first, body):
        first(Ring(0, 0, FIRST, None))
        with eng.Fori(0, HEADS - 2) as j:
            body(j, j // 4, Ring(len(FIRST), len(BODY), BODY, j), True, True)
        before = len(FIRST) + (HEADS - 2) * len(BODY)
        body(HEADS - 2, (HEADS - 2) // 4, Ring(before, 0, NEXT, 0), True, False)
        body(HEADS - 1, (HEADS - 1) // 4, Ring(before + len(NEXT), 0, LAST, 0), False, False)

    def next_pair(j):
        return (j + 1) // 4

    with stack, nc.Block() as block:
        @block.sync
        def _(sp):
            def load_w(j):
                if not (isinstance(j, int) and j == 0):
                    sp.wait_ge(b.w_lo, j)
                for u in range(2):
                    col = DH * j + 4 * DH * (j // 4) + 4 * DH * u
                    sp.dma_start(b.wr[:, :, u, :], w[:, :, bass.ds(col, DH)]).then_inc(b.w_in, 16)

            def swap(j, ring):
                wait_both(sp, ring.read(free, ("QB", 1)), ring.read(free, ("QB", 2)))
                rope_swap(sp, b.nql[:, 0:NS].bitcast(F32), b.q[:, 0:NS], b.qswap)

            def pair(ap, p):
                return ap[bass.ds(p, 1)]

            def keys_in(j, p):
                sp.dma_start(b.ks[:, :, :].bitcast(F32), pair(g.k_save, p).rearrange("o p m t -> (o p) m t")).then_inc(b.kv_in, 16)

            def values_in(p):
                sp.dma_start(b.v[:, :, :].rearrange("p c d -> p (c d)"), pair(g.v_save, p).rearrange("o p n -> (o p) n"))\
                    .then_inc(b.kv_in, 16)

            def first(ring):
                load_w(0)
                sp.dma_start(b.cos[:, :], a.rope_cos).then_inc(b.tab, 16)
                load_w(1)
                keys_in(0, 0)
                values_in(0)
                swap(0, ring)
                sp.wait_ge(b.rope, ROPE_STEPS)
                stack_queries(sp, b, b.qst)

            def body(j, p, ring, ahead1, ahead2):
                if ahead2:
                    load_w(j + 2)
                if ahead1:
                    sp.wait_ge(b.qst, 2 * STACK * j + 2 * STACK)
                    swap(j + 1, ring)
                    sp.wait_ge(b.s_mm, 2 * TILES * j + 2 * TILES)
                    keys_in(j + 1, next_pair(j))
                    sp.wait_ge(b.rope, ROPE_STEPS * j + 2 * ROPE_STEPS)
                    stack_queries(sp, b, b.qst)
                    sp.wait_ge(b.full, ring.done(("PV", 4)))
                    values_in(next_pair(j))

            chunks_of_q(sp, first, body)

        @block.scalar
        def _(act):
            def w_hi(j):
                act.wait_ge(b.w_in, 32 * j + 32)
                act.activation(b.wh[:, :, :], b.wr[:, :, :, :].rearrange("p k u d -> p k (u d)"), ACT.Copy).then_inc(b.w_hi, 1)

            def copy_out(ring, use, dst, cols, parts=1):
                act.wait_ge(b.full, ring.done(use))
                src = PS[:, ring.bank(use), 0:cols]
                act.activation(dst, src.rearrange("p (n t) -> p n t", n=parts) if parts > 1 else src, ACT.Copy)\
                    .then_inc(free[ring.bank(use)], 1)

            def project(ring, use):
                copy_out(ring, use, b.q[:, use[1] * NB:(use[1] + 1) * NB], NB)

            def squares(j):
                act.activation(sq, b.q[:, :], ACT.Square).then_inc(b.sq_d, 1)

            def softmax(j, t):
                for m in range(2):
                    act.wait_ge(b.nmax, 2 * (TILES * j + t) + m + 1)
                    act.activation(like_banks(b.e[:, m, t % 2, :], t), banks(g, m, t), ACT.Exp, bias=b.nb[:, m:m + 1],
                                   scale=SCALE, accum_out=b.l[:, m:m + 1]).then_inc(b.exp, 1)

            def first(ring):
                w_hi(0)
                for n in range(NN):
                    project(ring, ("W", n))
                for n in (1, 2):
                    ring.wait_read(act, free, ("W", n))
                squares(0)
                w_hi(1)
                for n in range(NN):
                    act.wait_ge(b.rope, ROPE_STEPS)
                    copy_out(ring, ("V", n), b.q[:, n * NB:(n + 1) * NB], NB)

            def body(j, p, ring, ahead1, ahead2):
                for s in range(STEPS):
                    if ahead1 and s == 0:
                        act.wait_ge(b.qst, 2 * STACK * j + 2 * STACK)
                        ring.wait_earlier_read(act, free)
                        squares(j + 1)
                    if ahead2 and s == 2:
                        w_hi(j + 2)
                    for use in step_uses(s, ahead1, ahead2):
                        if use[0] == "T" and use[2] == 0:
                            t, (c0, n) = use[1], groups_of(use[1])[use[3]]
                            dst = b.pt[:, 0, c0:c0 + n, (t % 2) * P:(t % 2 + 1) * P]
                            copy_out(ring, use, dst if n > 1 else dst[:, 0, :], n * P, n)
                    if s < TILES:
                        softmax(j, s)
                    for use in step_uses(s, ahead1, ahead2):
                        if use[0] == "PV":
                            n = PAIRS[use[1]][1] * P
                            act.wait_ge(b.y_out, 16 * (len(PAIRS) * j + use[1] + 1))
                            copy_out(ring, use, b.y[:, 0:n], n)
                        if use[0] == "W":
                            project(ring, use)

            chunks_of_q(act, first, body)

        @block.gpsimd
        def _(pool):
            def w_lo(j):
                pool.wait_ge(b.w_hi, j + 1)
                pool.tensor_tensor(b.wl[:, :, :], b.wr[:, :, :, :].rearrange("p k u d -> p k (u d)"), b.wh[:, :, :].bitcast(F32),
                                   ALU.subtract).then_inc(b.w_lo, 1)

            def root(ring):
                ring.wait_read(pool, free, ("QS",))
                pool.tensor_tensor(b.r[:, :, :].rearrange("p a b -> p (a b)"), b.ms[:, :, :].rearrange("p a b -> p (a b)"),
                                   g.half[:, 0:1].to_broadcast([P, 2 * TT]), ALU.pow).then_inc(b.r_d, 1)

            def first(ring):
                pool.dma_start(b.sin[:, :], a.rope_sin).then_inc(b.y_out, 16)
                pool.memset(b.rl[:, :], 0.0).then_inc(b.prob, 1)
                w_lo(0)
                root(ring)
                w_lo(1)

            def body(j, p, ring, ahead1, ahead2):
                for s in range(STEPS):
                    if s < TILES:
                        pool.wait_ge(b.rl_d, TILES * j + s + 1)
                        pool.tensor_tensor(b.mark[:, :], b.rl[:, 0:1], b.rl[:, 1:2], ALU.mult)
                        for m in range(2):
                            e = b.e[:, m, s % 2, 0:keys(s)]
                            pool.tensor_scalar(e, e, b.rl[:, m:m + 1], None, ALU.mult).then_inc(b.prob, 1)
                    if ahead1 and s == 1:
                        root(ring)
                    if ahead2 and s == 2:
                        w_lo(j + 2)
                    for use in step_uses(s, ahead1, ahead2):
                        if use[0] == "PV":
                            t0, n = PAIRS[use[1]]
                            ring.wait_read(pool, free, use)
                            pool.dma_start(g.o_save[bass.ds(j, 1), :, t0 * P:(t0 + n) * P].rearrange("o p t -> (o p) t"),
                                           b.y[:, 0:n * P]).then_inc(b.y_out, 16)

            chunks_of_q(pool, first, body)
            pool.wait_ge(b.y_out, 16 * len(PAIRS) * HEADS + 16)

        @block.tensor
        def _(pe):
            def do(ring, j, use):
                what, bank = use[0], ring.bank(use)
                ring.wait_free(pe, free, use)
                out = PS[:, bank, :]
                if what in "WV":
                    if use[1] == 0:
                        pe.wait_ge(b.w_lo, (j + 3 if ring.head is not None else 1 + (what == "V")))
                    last = linear_bank(g, pe, bank, b.wh, b.wl, use[1])
                elif what == "QS":
                    pe.wait_ge(b.sq_d, j + 2 if ring.head is not None else 1)
                    for t in range(TT):
                        last = pe.matmul(out[:, 2 * t:2 * t + 2], sq[:, t * P:(t + 1) * P], g.ones_h[:, :], start=True, stop=True)
                elif what == "QB":
                    pe.wait_ge(b.r_d, j + 2 if ring.head is not None else 1)
                    for i in range(3):
                        last = broadcast_heads(g, pe, out[:, i * P:(i + 1) * P], b.r[:, 3 * use[1] + i, :])
                elif what == "T":
                    _, t, m, i = use
                    if i == 0:
                        pe.wait_ge(b.prob, 2 * (TILES * j + t) + m + 2)
                    c0, n = groups_of(t)[i]
                    last = transposes(g, pe, bank, b.e[:, m, t % 2, :], c0, n)
                elif what == "PV":
                    t0, n = PAIRS[use[1]]
                    t = t0 + n - 1
                    for m in range(2):
                        ring.wait_read(pe, free, ("T", t, m, len(groups_of(t)) - 1))
                    nk = keys(t0) // P
                    for c in range(nk):
                        for m in range(2):
                            last = pe.matmul(out[m * DH:(m + 1) * DH, 0:n * P], b.v[:, value_chunk(t0, c), m * DH:(m + 1) * DH],
                                             b.pt[:, m, c, 0:n * P], start=c == 0, stop=c == nk - 1)
                last.then_inc(b.full, 1)

            def first(ring):
                for use in FIRST:
                    do(ring, 0, use)

            def body(j, p, ring, ahead1, ahead2):
                for s in range(STEPS):
                    if s == 0:
                        pe.wait_ge(b.kv_in, 32 * j + 32)
                        pe.wait_ge(b.qst, 2 * STACK * j + 2 * STACK)
                    for m in range(2):
                        if s < TILES:
                            if s:
                                pe.wait_ge(b.exp, 2 * (TILES * j + s) + m - 1)
                            scores(g, pe, b, m, s).then_inc(b.s_mm, 1)
                    for use in step_uses(s, ahead1, ahead2):
                        do(ring, j, use)

            chunks_of_q(pe, first, body)

        @block.vector
        def _(dve):
            def mean_square(ring):
                dve.wait_ge(b.full, ring.done(("QS",)))
                dve.tensor_scalar(b.ms[:, :, :].rearrange("p a b -> p (a b)"), PS[:, ring.bank(("QS",)), 0:2 * TT], EPS, None,
                                  ALU.add).then_inc(free[ring.bank(("QS",))], 1)

            def normalise(ring):
                for n in range(NN):
                    use, s = ("QB", n), slice(n * NB, (n + 1) * NB)
                    dve.wait_ge(b.full, ring.done(use))
                    dve.scalar_tensor_tensor(b.q[:, s], b.q[:, s], g.par[:, PC_QN:PC_QN + 1], PS[:, ring.bank(use), 0:NB],
                                             ALU.mult, ALU.mult).then_inc(free[ring.bank(use)], 1)

            def rope(j):
                dve.wait_ge(b.qswap, SWAP * j + SWAP)
                rotate_and_split(Chain(dve, b.rope, ROPE_STEPS * j), dve, b.q, b.nql, b.nqh, 0, T, b.cos, b.sin)

            dve.wait_ge(b.tab, 16)
            dve.wait_ge(b.y_out, 16)

            def first(ring):
                mean_square(ring)
                normalise(ring)
                rope(0)

            def body(j, p, ring, ahead1, ahead2):
                for s in range(STEPS):
                    if s < TILES:
                        link = Chain(dve, b.soft, 2 * (TILES * j + s))
                        for m in range(2):
                            dve.wait_ge(b.s_mm, 2 * (TILES * j + s) + m + 1)
                            link(dve.reduce_max(b.mx[:, m:m + 1], banks(g, m, s), AX.XY if s < QT else AX.X))
                            dve.tensor_scalar(b.nb[:, m:m + 1], b.mx[:, m:m + 1], -SCALE, None, ALU.mult).then_inc(b.nmax, 1)
                    for use in step_uses(s, ahead1, ahead2):
                        if use[0] == "T" and use[2] == 1:
                            t, (c0, n) = use[1], groups_of(use[1])[use[3]]
                            dve.wait_ge(b.full, ring.done(use))
                            dst, src = b.pt[:, 1, c0:c0 + n, (t % 2) * P:(t % 2 + 1) * P], PS[:, ring.bank(use), 0:n * P]
                            if t % 2 == 0 and use[3] == 0:
                                if t:
                                    dve.wait_ge(b.full, ring.done(("PV", t // 2 - 1)))
                            dve.tensor_copy(dst, src.rearrange("p (c q) -> p c q", c=n)).then_inc(free[ring.bank(use)], 1)
                    if s < TILES:
                        dve.wait_ge(b.exp, 2 * (TILES * j + s) + 2)
                        dve.wait_ge(b.prob, 2 * (TILES * j + s) + 1)
                        dve.reciprocal(b.rl[:, :], b.l[:, :]).then_inc(b.rl_d, 1)
                    if ahead1 and s == 1:
                        mean_square(ring)
                    if ahead1 and s == 3:
                        normalise(ring)
                    if ahead1 and s == 6:
                        rope(j + 1)

            chunks_of_q(dve, first, body)


INPUTS = ["x_prompt", "x_sample", "cache_k_diff", "cache_v_diff", "cache_k_gqa", "cache_v_gqa", "c", "c_ctx", "mod_w",
          "mod_b", "norm_attn", "norm_ffn", "w_qkv_diff", "w_o_diff", "lambda_diff", "subln_diff", "w_qkv_gqa",
          "w_o_gqa", "q_norm_gqa", "k_norm_gqa", "w_up", "conv_w", "conv_b", "w_down", "final_norm"]
OUTPUTS = {"y_prompt": (1, NP, D), "y_sample": (1, NS, D), "new_k_diff": (1, 1, 8, NP, P), "new_v_diff": (1, 1, 8, NP, P),
           "new_k_gqa": (1, 1, 4, NP, DH), "new_v_gqa": (1, 1, 4, NP, DH)}


def kernel(**inputs):
    import concourse.bacc as bacc
    from concourse.bass_utils import run_bass_kernel_spmd

    nc = bacc.Bacc("TRN2", target_bir_lowering=False, num_devices=1)
    arrays = {n: np.ascontiguousarray(inputs[n]) for n in INPUTS}
    arrays["rope_cos"], arrays["rope_sin"] = rope_tables()
    tensors = {n: nc.dram_tensor(n, v.shape, F32, kind="ExternalInput").ap() for n, v in arrays.items()}
    for n, shape in OUTPUTS.items():
        tensors[n] = nc.dram_tensor(n, shape, F32, kind="ExternalOutput").ap()
    build(nc, namedtuple("Arrays", tensors)(**tensors))
    r = run_bass_kernel_spmd(nc, [arrays], core_ids=[0])
    return tuple(r.results[0][n] for n in OUTPUTS)
```
